# Optimizing a Trainium2 kernel written in Bass

```python
import jax, jax.numpy as jnp
from jax import lax
import numpy as np

D_MODEL = 1024
BATCH = 1
SEQ = 256
DEPTH = 2

GRID_W = 64
CTX_LEN = 256
N_MIXERS = 2
N_GLA_LAYERS = (DEPTH + 1) // 2
N_MLA_LAYERS = DEPTH // 2
EPS = 1e-6

GLA_HEADS = 4
GLA_DK = D_MODEL // 2 // GLA_HEADS
GLA_DV = D_MODEL // GLA_HEADS
GLA_GATE_RANK = 16
GLA_GATE_NORMALIZER = 16.0
GLA_CHUNK = 64
GLA_IN = 2 * GLA_HEADS * GLA_DK + 2 * GLA_HEADS * GLA_DV

MLA_HEADS = 8
MLA_NOPE = 128
MLA_ROPE = 64
MLA_QK = MLA_NOPE + MLA_ROPE
MLA_V = 128
MLA_Q_RANK = 384
MLA_KV_RANK = 256
MLA_DOWN = MLA_Q_RANK + MLA_KV_RANK + MLA_ROPE
ROPE_THETA = 10000.0
ROPE_FREQS = MLA_ROPE // 4
Q_BLOCK = 128

D_FF = 2816
CONV_W = 3


def rmsnorm(x, g):
    xf = x.astype(jnp.float32)
    y = xf * lax.rsqrt(jnp.mean(xf * xf, axis=-1, keepdims=True) + EPS)
    return (y * g.astype(jnp.float32)).astype(x.dtype)

def ada_modulation(cond, w, b):
    m = jax.nn.silu(cond) @ w + b
    return jnp.split(m, 6, axis=-1)

def modulate(x, g, shift, scale):
    return rmsnorm(x, g) * (1 + scale[..., None, :]) + shift[..., None, :]

def axial_rope_tables(length):
    rows = length // GRID_W
    t = jnp.arange(rows * GRID_W)
    row = (t // GRID_W).astype(jnp.float32)
    col = (t % GRID_W).astype(jnp.float32)
    inv = ROPE_THETA ** (-jnp.arange(ROPE_FREQS, dtype=jnp.float32) / ROPE_FREQS)
    ang = jnp.stack([row[:, None] * inv, col[:, None] * inv], axis=1)
    return jnp.cos(ang)[:, None], jnp.sin(ang)[:, None]

def apply_axial_rope(x, cos, sin):
    xr = x.astype(jnp.float32).reshape(*x.shape[:-1], 2, 2, ROPE_FREQS)
    x1, x2 = xr[..., 0, :], xr[..., 1, :]
    out = jnp.stack([x1 * cos - x2 * sin, x1 * sin + x2 * cos], axis=-2)
    return out.reshape(x.shape).astype(x.dtype)

def gla_project(h, w_in):
    B, L, _ = h.shape
    q, k, v, r = jnp.split(h @ w_in, [GLA_HEADS * GLA_DK, 2 * GLA_HEADS * GLA_DK,
                                      2 * GLA_HEADS * GLA_DK + GLA_HEADS * GLA_DV], axis=-1)
    q = q.reshape(B, L, GLA_HEADS, GLA_DK) * (GLA_DK ** -0.5)
    k = k.reshape(B, L, GLA_HEADS, GLA_DK)
    v = v.reshape(B, L, GLA_HEADS, GLA_DV)
    return q, k, v, r

def gla_log_decay(h, w1, w2, b):
    z = ((h @ w1) @ w2 + b).astype(jnp.float32)
    return (jax.nn.log_sigmoid(z) / GLA_GATE_NORMALIZER).reshape(*h.shape[:-1], GLA_HEADS, GLA_DK)

def gla_chunked(q, k, v, g, s0):
    B, L, H, _ = q.shape
    n = L // GLA_CHUNK
    def chunks(a):
        return a.reshape(B, n, GLA_CHUNK, H, a.shape[-1]).astype(jnp.float32)
    qc, kc, vc, gc = chunks(q), chunks(k), chunks(v), chunks(g)
    b = jnp.cumsum(gc, axis=2)
    b_last = b[:, :, -1:]
    q_dec = qc * jnp.exp(b)
    k_intra = kc * jnp.exp(-b)
    k_state = kc * jnp.exp(b_last - b)
    mask = jnp.tril(jnp.ones((GLA_CHUNK, GLA_CHUNK), dtype=bool))
    scores = jnp.where(mask, jnp.einsum('bnthd,bnshd->bnhts', q_dec, k_intra), 0.0)
    o_intra = jnp.einsum('bnhts,bnshv->bnthv', scores, vc)

    def step(S, xs):
        qd, ks, vv, bl = xs
        o = jnp.einsum('bthd,bhdv->bthv', qd, S)
        S = S * jnp.exp(bl)[..., None] + jnp.einsum('bthd,bthv->bhdv', ks, vv)
        return S, o

    xs = (jnp.moveaxis(q_dec, 1, 0), jnp.moveaxis(k_state, 1, 0),
          jnp.moveaxis(vc, 1, 0), jnp.moveaxis(b_last[:, :, 0], 1, 0))
    s_final, o_inter = lax.scan(step, s0.astype(jnp.float32), xs)
    o = o_intra + jnp.moveaxis(o_inter, 0, 1)
    return o.reshape(B, L, H, v.shape[-1]).astype(v.dtype), s_final

def gla_bidirectional(q, k, v, g_fwd, g_bwd, s_fwd0, s_bwd0):
    o_f, s_f = gla_chunked(q, k, v, g_fwd, s_fwd0)
    flip = lambda a: jnp.flip(a, axis=1)
    o_b, s_b = gla_chunked(flip(q), flip(k), flip(v), flip(g_bwd), s_bwd0)
    return o_f + flip(o_b), s_f, s_b

def gla_output(o, r, out_norm, w_out):
    B, L = o.shape[:2]
    o = rmsnorm(o, out_norm).reshape(B, L, GLA_HEADS * GLA_DV)
    return (o * jax.nn.silu(r)) @ w_out

def gla_mixer(h, hc, w_in, gate_w1, gate_w2, gate_b, out_norm, w_out, need_ctx_out):
    B = h.shape[0]
    s0 = jnp.zeros((B, GLA_HEADS, GLA_DK, GLA_DV), jnp.float32)
    qc, kc, vc, rc = gla_project(hc, w_in)
    gfc = gla_log_decay(hc, gate_w1[0], gate_w2[0], gate_b[0])
    gbc = gla_log_decay(hc, gate_w1[1], gate_w2[1], gate_b[1])
    oc, s_fwd, s_bwd = gla_bidirectional(qc, kc, vc, gfc, gbc, s0, s0)
    q, k, v, r = gla_project(h, w_in)
    gf = gla_log_decay(h, gate_w1[0], gate_w2[0], gate_b[0])
    gb = gla_log_decay(h, gate_w1[1], gate_w2[1], gate_b[1])
    o, _, _ = gla_bidirectional(q, k, v, gf, gb, s_fwd, s_bwd)
    out = gla_output(o, r, out_norm, w_out)
    out_c = gla_output(oc, rc, out_norm, w_out) if need_ctx_out else None
    return out, out_c

def split_norm(t, g):
    return jnp.concatenate([rmsnorm(t[..., :MLA_NOPE], g[:MLA_NOPE]),
                            rmsnorm(t[..., MLA_NOPE:], g[MLA_NOPE:])], axis=-1)

def mla_qkv(h, w_down, q_lora_norm, kv_lora_norm, w_uq, w_ukv, q_norm, k_norm, rope, want_q):
    B, L, _ = h.shape
    c_q, c_kv, k_pe = jnp.split(h @ w_down, [MLA_Q_RANK, MLA_Q_RANK + MLA_KV_RANK], axis=-1)
    kv = (rmsnorm(c_kv, kv_lora_norm) @ w_ukv).reshape(B, L, MLA_HEADS, MLA_NOPE + MLA_V)
    k_nope, v = kv[..., :MLA_NOPE], kv[..., MLA_NOPE:]
    k_nope = rmsnorm(k_nope, k_norm[:MLA_NOPE])
    k_pe = rmsnorm(k_pe, k_norm[MLA_NOPE:])[:, :, None, :]
    if rope is not None:
        k_pe = apply_axial_rope(k_pe, *rope)
    k = jnp.concatenate([k_nope, jnp.broadcast_to(k_pe, (B, L, MLA_HEADS, MLA_ROPE))], axis=-1)
    q = None
    if want_q:
        q = split_norm((rmsnorm(c_q, q_lora_norm) @ w_uq).reshape(B, L, MLA_HEADS, MLA_QK), q_norm)
        if rope is not None:
            q = jnp.concatenate([q[..., :MLA_NOPE], apply_axial_rope(q[..., MLA_NOPE:], *rope)], axis=-1)
    return q, k, v

def block_softmax_attention(q, k, v):
    B, L, H, Dh = q.shape
    nb = L // Q_BLOCK
    scale = Dh ** -0.5
    qb = jnp.moveaxis(q.reshape(B, nb, Q_BLOCK, H, Dh), 1, 0)
    def one(qblk):
        s = jnp.einsum('bqhd,bkhd->bhqk', qblk, k).astype(jnp.float32) * scale
        p = jax.nn.softmax(s, axis=-1).astype(v.dtype)
        return jnp.einsum('bhqk,bkhv->bqhv', p, v)
    o = lax.map(one, qb)
    return jnp.moveaxis(o, 0, 1).reshape(B, L, H, v.shape[-1])

def mla_mixer(h, hc, w_down, q_lora_norm, kv_lora_norm, w_uq, w_ukv, q_norm, k_norm, w_out, rope, need_ctx_out):
    B, L, _ = h.shape
    qc, kc, vc = mla_qkv(hc, w_down, q_lora_norm, kv_lora_norm, w_uq, w_ukv, q_norm, k_norm, None, need_ctx_out)
    q, k, v = mla_qkv(h, w_down, q_lora_norm, kv_lora_norm, w_uq, w_ukv, q_norm, k_norm, rope, True)
    o = block_softmax_attention(q, jnp.concatenate([kc, k], axis=1), jnp.concatenate([vc, v], axis=1))
    out = o.reshape(B, L, MLA_HEADS * MLA_V) @ w_out
    out_c = None
    if need_ctx_out:
        oc = block_softmax_attention(qc, kc, vc)
        out_c = oc.reshape(B, hc.shape[1], MLA_HEADS * MLA_V) @ w_out
    return out, out_c

def depthwise_conv3(u, w, b):
    up = jnp.pad(u, ((0, 0), (1, 1), (0, 0)))
    return up[:, :-2] * w[0] + up[:, 1:-1] * w[1] + up[:, 2:] * w[2] + b

def conv_ffn(h, w_up, conv_w, conv_b, w_down):
    u = depthwise_conv3(h @ w_up, conv_w, conv_b)
    a, g = jnp.split(u, 2, axis=-1)
    return (jax.nn.silu(g) * a) @ w_down

def first_inputs(seed: int = 0) -> dict:
    key = jax.random.key(seed)
    ks = jax.random.split(key, 32)
    nrm = lambda k, shape, s: jax.random.normal(k, shape, jnp.float32) * s
    gain = lambda k, shape: 1.0 + 0.05 * jax.random.normal(k, shape, jnp.float32)
    return {
        'x': nrm(ks[0], (BATCH, SEQ, D_MODEL), 1.0),
        'c': nrm(ks[1], (BATCH, D_MODEL), 1.0),
        'ctx': nrm(ks[2], (BATCH, CTX_LEN, D_MODEL), 1.0),
        'c_ctx': nrm(ks[3], (D_MODEL,), 1.0),
        'w_ada': nrm(ks[4], (DEPTH, D_MODEL, 6 * D_MODEL), 0.5 * D_MODEL ** -0.5),
        'b_ada': nrm(ks[5], (DEPTH, 6 * D_MODEL), 0.02),
        'norm_mix': gain(ks[6], (DEPTH, D_MODEL)),
        'norm_ffn': gain(ks[7], (DEPTH, D_MODEL)),
        'gla_w_in': nrm(ks[8], (N_GLA_LAYERS, D_MODEL, GLA_IN), D_MODEL ** -0.5),
        'gla_gate_w1': nrm(ks[9], (N_GLA_LAYERS, 2, D_MODEL, GLA_GATE_RANK), D_MODEL ** -0.5),
        'gla_gate_w2': nrm(ks[10], (N_GLA_LAYERS, 2, GLA_GATE_RANK, GLA_HEADS * GLA_DK), GLA_GATE_RANK ** -0.5),
        'gla_gate_b': nrm(ks[11], (N_GLA_LAYERS, 2, GLA_HEADS * GLA_DK), 0.1),
        'gla_out_norm': gain(ks[12], (N_GLA_LAYERS, GLA_DV)),
        'gla_w_out': nrm(ks[13], (N_GLA_LAYERS, GLA_HEADS * GLA_DV, D_MODEL), (GLA_HEADS * GLA_DV) ** -0.5),
        'mla_w_down': nrm(ks[14], (N_MLA_LAYERS, D_MODEL, MLA_DOWN), D_MODEL ** -0.5),
        'mla_q_lora_norm': gain(ks[15], (N_MLA_LAYERS, MLA_Q_RANK)),
        'mla_kv_lora_norm': gain(ks[16], (N_MLA_LAYERS, MLA_KV_RANK)),
        'mla_w_uq': nrm(ks[17], (N_MLA_LAYERS, MLA_Q_RANK, MLA_HEADS * MLA_QK), MLA_Q_RANK ** -0.5),
        'mla_w_ukv': nrm(ks[18], (N_MLA_LAYERS, MLA_KV_RANK, MLA_HEADS * (MLA_NOPE + MLA_V)), MLA_KV_RANK ** -0.5),
        'mla_q_norm': gain(ks[19], (N_MLA_LAYERS, MLA_QK)),
        'mla_k_norm': gain(ks[20], (N_MLA_LAYERS, MLA_QK)),
        'mla_w_out': nrm(ks[21], (N_MLA_LAYERS, MLA_HEADS * MLA_V, D_MODEL), (MLA_HEADS * MLA_V) ** -0.5),
        'ffn_w_up': nrm(ks[22], (DEPTH, D_MODEL, 2 * D_FF), D_MODEL ** -0.5),
        'ffn_conv_w': nrm(ks[23], (DEPTH, CONV_W, 2 * D_FF), CONV_W ** -0.5),
        'ffn_conv_b': nrm(ks[24], (DEPTH, 2 * D_FF), 0.02),
        'ffn_w_down': nrm(ks[25], (DEPTH, D_FF, D_MODEL), D_FF ** -0.5),
    }

def first_block(x, c, ctx, c_ctx, w_ada, b_ada, norm_mix, norm_ffn,
              gla_w_in, gla_gate_w1, gla_gate_w2, gla_gate_b, gla_out_norm, gla_w_out,
              mla_w_down, mla_q_lora_norm, mla_kv_lora_norm, mla_w_uq, mla_w_ukv,
              mla_q_norm, mla_k_norm, mla_w_out,
              ffn_w_up, ffn_conv_w, ffn_conv_b, ffn_w_down):
    rope = axial_rope_tables(x.shape[1])
    xc = ctx
    for i in range(DEPTH):
        last = i == DEPTH - 1
        j = i // N_MIXERS
        sh1, sc1, g1, sh2, sc2, g2 = ada_modulation(c, w_ada[i], b_ada[i])
        csh1, csc1, cg1, csh2, csc2, cg2 = ada_modulation(c_ctx, w_ada[i], b_ada[i])
        h = modulate(x, norm_mix[i], sh1, sc1)
        hc = modulate(xc, norm_mix[i], csh1, csc1)
        if i % N_MIXERS == 0:
            o, oc = gla_mixer(h, hc, gla_w_in[j], gla_gate_w1[j], gla_gate_w2[j], gla_gate_b[j],
                              gla_out_norm[j], gla_w_out[j], not last)
        else:
            o, oc = mla_mixer(h, hc, mla_w_down[j], mla_q_lora_norm[j], mla_kv_lora_norm[j],
                              mla_w_uq[j], mla_w_ukv[j], mla_q_norm[j], mla_k_norm[j], mla_w_out[j],
                              rope, not last)
        x = x + g1[:, None, :] * o
        x = x + g2[:, None, :] * conv_ffn(modulate(x, norm_ffn[i], sh2, sc2),
                                          ffn_w_up[i], ffn_conv_w[i], ffn_conv_b[i], ffn_w_down[i])
        if not last:
            xc = xc + cg1 * oc
            xc = xc + cg2 * conv_ffn(modulate(xc, norm_ffn[i], csh2, csc2),
                                     ffn_w_up[i], ffn_conv_w[i], ffn_conv_b[i], ffn_w_down[i])
    return x


DEPTH_2 = 1

HEAD_DIM = 64
ATTN_HEADS = 8
ATTN_W = ATTN_HEADS * HEAD_DIM
CONV_W_2 = 256
MEM_HEADS = 4
MEM_W = MEM_HEADS * HEAD_DIM
MIX_W = ATTN_W + CONV_W_2 + MEM_W
N_MEM = 256
DILATED_PATTERNS = ((128, 1), (512, 4), (2048, 16))
ROPE_THETA_2 = 500000.0
ROT_DIM = HEAD_DIM // 4
CONV_K = 31
FFN_CONV_K = 3
IN_COLS = 3 * ATTN_W + 2 * CONV_W_2 + MEM_W
SPLITS = (ATTN_W, 2 * ATTN_W, 3 * ATTN_W, 3 * ATTN_W + 2 * CONV_W_2)
NORM_EPS = 1e-6
NEG_INF = -1e30


def rms_norm(x, g):
    xf = x.astype(jnp.float32)
    y = xf * lax.rsqrt(jnp.mean(xf * xf, axis=-1, keepdims=True) + NORM_EPS)
    return (y * g.astype(jnp.float32)).astype(x.dtype)

def layer_norm(x, g, b):
    xf = x.astype(jnp.float32)
    mu = jnp.mean(xf, axis=-1, keepdims=True)
    var = jnp.mean(jnp.square(xf - mu), axis=-1, keepdims=True)
    y = (xf - mu) * lax.rsqrt(var + NORM_EPS)
    return (y * g.astype(jnp.float32) + b.astype(jnp.float32)).astype(x.dtype)

def partial_rotary(x, positions):
    inv_freq = ROPE_THETA_2 ** (-jnp.arange(0, ROT_DIM, 2, dtype=jnp.float32) / ROT_DIM)
    ang = positions.astype(jnp.float32)[..., None] * inv_freq
    cos = jnp.cos(ang)[:, :, None, :]
    sin = jnp.sin(ang)[:, :, None, :]
    xr = x[..., :ROT_DIM].astype(jnp.float32)
    x1, x2 = xr[..., : ROT_DIM // 2], xr[..., ROT_DIM // 2:]
    rot = jnp.concatenate([x1 * cos - x2 * sin, x2 * cos + x1 * sin], axis=-1)
    return jnp.concatenate([rot.astype(x.dtype), x[..., ROT_DIM:]], axis=-1)

def depthwise_conv(x, w, b):
    k = w.shape[0]
    y = lax.conv_general_dilated(
        x, w[:, None, :].astype(x.dtype), window_strides=(1,),
        padding=[(k // 2, k // 2)], dimension_numbers=("NWC", "WIO", "NWC"),
        feature_group_count=x.shape[-1])
    return y + b.astype(x.dtype)

def banded_attention(q, k, v, half):
    n, L, H, Dh = q.shape
    blk = half
    nb = -(-L // blk)
    Lp = nb * blk
    qb = jnp.pad(q, ((0, 0), (0, Lp - L), (0, 0), (0, 0))).reshape(n, nb, blk, H, Dh)

    def halo(t):
        tp = jnp.pad(t, ((0, 0), (blk, Lp - L + blk), (0, 0), (0, 0))).reshape(n, nb + 2, blk, H, Dh)
        return jnp.concatenate([tp[:, :-2], tp[:, 1:-1], tp[:, 2:]], axis=2)

    kb, vb = halo(k), halo(v)
    s = jnp.einsum("nbqhd,nbkhd->nbhqk", qb, kb).astype(jnp.float32) * (Dh ** -0.5)
    bidx = jnp.arange(nb)[:, None, None]
    qi = jnp.arange(blk)[None, :, None]
    kj = jnp.arange(3 * blk)[None, None, :]
    key_pos = bidx * blk - blk + kj
    valid = (jnp.abs(kj - blk - qi) <= half) & (key_pos >= 0) & (key_pos < L)
    s = jnp.where(valid[None, :, None], s, NEG_INF)
    m = jnp.max(s, axis=-1, keepdims=True)
    p = jnp.exp(s - m)
    den = jnp.sum(p, axis=-1, keepdims=True)
    o = jnp.einsum("nbhqk,nbkhd->nbqhd", p, vb.astype(jnp.float32))
    o = o / jnp.transpose(den, (0, 1, 3, 2, 4))
    lse = jnp.transpose((m + jnp.log(den))[..., 0], (0, 1, 3, 2))
    return o.reshape(n, Lp, H, Dh)[:, :L], lse.reshape(n, Lp, H)[:, :L]

def dilated_attention(q, k, v, window, dil):
    B, S, H, Dh = q.shape
    L = S // dil

    def to_sub(t):
        return t.reshape(B, L, dil, H, Dh).transpose(0, 2, 1, 3, 4).reshape(B * dil, L, H, Dh)

    o, lse = banded_attention(to_sub(q), to_sub(k), to_sub(v), window // (2 * dil))
    o = o.reshape(B, dil, L, H, Dh).transpose(0, 2, 1, 3, 4).reshape(B, S, H, Dh)
    lse = lse.reshape(B, dil, L, H).transpose(0, 2, 1, 3).reshape(B, S, H)
    return o, lse

def second_inputs(seed: int = 0) -> dict:
    key = jax.random.key(seed)
    ks = jax.random.split(key, 24)
    f32 = jnp.float32

    def nrm(k, shape, scale):
        return jax.random.normal(k, shape, f32) * scale

    def gain(k, shape):
        return 1.0 + 0.02 * jax.random.normal(k, shape, f32)

    offsets = jax.random.randint(ks[2], (BATCH, 1), 0, 1024, dtype=jnp.int32)
    positions = (jnp.arange(SEQ, dtype=jnp.int32)[None, :] + offsets).astype(jnp.int32)
    return {
        "x": nrm(ks[0], (BATCH, SEQ, D_MODEL), 1.0),
        "mem": nrm(ks[1], (BATCH, N_MEM, D_MODEL), 1.0),
        "positions": positions,
        "mix_norm_g": gain(ks[3], (DEPTH_2, D_MODEL)),
        "mem_norm_g": gain(ks[4], (DEPTH_2, D_MODEL)),
        "w_in": nrm(ks[5], (DEPTH_2, D_MODEL, IN_COLS), D_MODEL ** -0.5),
        "w_mem_kv": nrm(ks[6], (DEPTH_2, D_MODEL, 2 * MEM_W), D_MODEL ** -0.5),
        "q_norm_g": gain(ks[7], (DEPTH_2, HEAD_DIM)),
        "k_norm_g": gain(ks[8], (DEPTH_2, HEAD_DIM)),
        "mq_norm_g": gain(ks[9], (DEPTH_2, HEAD_DIM)),
        "mk_norm_g": gain(ks[10], (DEPTH_2, HEAD_DIM)),
        "conv_dw_w": nrm(ks[11], (DEPTH_2, CONV_K, CONV_W_2), CONV_K ** -0.5),
        "conv_dw_b": nrm(ks[12], (DEPTH_2, CONV_W_2), 0.02),
        "conv_ln_g": gain(ks[13], (DEPTH_2, CONV_W_2)),
        "conv_ln_b": nrm(ks[14], (DEPTH_2, CONV_W_2), 0.02),
        "w_out": nrm(ks[15], (DEPTH_2, MIX_W, D_MODEL), MIX_W ** -0.5),
        "ffn_norm_g": gain(ks[16], (DEPTH_2, D_MODEL)),
        "w_up": nrm(ks[17], (DEPTH_2, D_MODEL, 2 * D_FF), D_MODEL ** -0.5),
        "ffn_dw_w": nrm(ks[18], (DEPTH_2, FFN_CONV_K, 2 * D_FF), FFN_CONV_K ** -0.5),
        "ffn_dw_b": nrm(ks[19], (DEPTH_2, 2 * D_FF), 0.02),
        "w_down": nrm(ks[20], (DEPTH_2, D_FF, D_MODEL), D_FF ** -0.5),
    }

def second_block(x, mem, positions, mix_norm_g, mem_norm_g, w_in, w_mem_kv, q_norm_g, k_norm_g,
              mq_norm_g, mk_norm_g, conv_dw_w, conv_dw_b, conv_ln_g, conv_ln_b, w_out,
              ffn_norm_g, w_up, ffn_dw_w, ffn_dw_b, w_down):
    B, S, _ = x.shape
    h = x
    for l in range(DEPTH_2):
        hn = rms_norm(h, mix_norm_g[l])
        proj = hn @ w_in[l]
        q, k, v, glu, qm = jnp.split(proj, SPLITS, axis=-1)

        q = partial_rotary(rms_norm(q.reshape(B, S, ATTN_HEADS, HEAD_DIM), q_norm_g[l]), positions)
        k = partial_rotary(rms_norm(k.reshape(B, S, ATTN_HEADS, HEAD_DIM), k_norm_g[l]), positions)
        v = v.reshape(B, S, ATTN_HEADS, HEAD_DIM)
        outs, lses = [], []
        for window, dil in DILATED_PATTERNS:
            o, lse = dilated_attention(q, k, v, window, dil)
            outs.append(o)
            lses.append(lse)
        wts = jax.nn.softmax(jnp.stack(lses, axis=0), axis=0)
        attn = jnp.sum(wts[..., None] * jnp.stack(outs, axis=0), axis=0)
        attn = attn.astype(h.dtype).reshape(B, S, ATTN_W)

        ga, gg = jnp.split(glu, 2, axis=-1)
        c = ga * jax.nn.sigmoid(gg)
        c = depthwise_conv(c, conv_dw_w[l], conv_dw_b[l])
        c = jax.nn.silu(layer_norm(c, conv_ln_g[l], conv_ln_b[l]))

        qm = rms_norm(qm.reshape(B, S, MEM_HEADS, HEAD_DIM), mq_norm_g[l])
        kvm = rms_norm(mem, mem_norm_g[l]) @ w_mem_kv[l]
        km, vm = jnp.split(kvm, 2, axis=-1)
        km = rms_norm(km.reshape(B, N_MEM, MEM_HEADS, HEAD_DIM), mk_norm_g[l])
        vm = vm.reshape(B, N_MEM, MEM_HEADS, HEAD_DIM)
        sm = jnp.einsum("bshd,bmhd->bhsm", qm, km).astype(jnp.float32) * (HEAD_DIM ** -0.5)
        pm = jax.nn.softmax(sm, axis=-1)
        mo = jnp.einsum("bhsm,bmhd->bshd", pm, vm.astype(jnp.float32))
        mo = mo.astype(h.dtype).reshape(B, S, MEM_W)

        mixed = jnp.concatenate([attn, c, mo], axis=-1)
        h = h + mixed @ w_out[l]

        f = rms_norm(h, ffn_norm_g[l]) @ w_up[l]
        f = depthwise_conv(f, ffn_dw_w[l], ffn_dw_b[l])
        fg, fu = jnp.split(f, 2, axis=-1)
        h = h + (jax.nn.silu(fg) * fu) @ w_down[l]
    return h


def setup_inputs(seed=0):
    out = dict(first_inputs(seed))
    for name, value in second_inputs(seed + 1).items():
        if name != "x":
            out[name + "_2"] = value
    return out


def reference(
    x, c, ctx, c_ctx, w_ada, b_ada, norm_mix, norm_ffn, gla_w_in, gla_gate_w1, gla_gate_w2,
    gla_gate_b, gla_out_norm, gla_w_out, mla_w_down, mla_q_lora_norm, mla_kv_lora_norm,
    mla_w_uq, mla_w_ukv, mla_q_norm, mla_k_norm, mla_w_out, ffn_w_up, ffn_conv_w, ffn_conv_b,
    ffn_w_down, mem_2, positions_2, mix_norm_g_2, mem_norm_g_2, w_in_2, w_mem_kv_2, q_norm_g_2,
    k_norm_g_2, mq_norm_g_2, mk_norm_g_2, conv_dw_w_2, conv_dw_b_2, conv_ln_g_2, conv_ln_b_2,
    w_out_2, ffn_norm_g_2, w_up_2, ffn_dw_w_2, ffn_dw_b_2, w_down_2,
):
    x = first_block(
        x, c, ctx, c_ctx, w_ada, b_ada, norm_mix, norm_ffn, gla_w_in, gla_gate_w1, gla_gate_w2,
        gla_gate_b, gla_out_norm, gla_w_out, mla_w_down, mla_q_lora_norm, mla_kv_lora_norm,
        mla_w_uq, mla_w_ukv, mla_q_norm, mla_k_norm, mla_w_out, ffn_w_up, ffn_conv_w,
        ffn_conv_b, ffn_w_down,
    )
    return second_block(
        x, mem_2, positions_2, mix_norm_g_2, mem_norm_g_2, w_in_2, w_mem_kv_2, q_norm_g_2,
        k_norm_g_2, mq_norm_g_2, mk_norm_g_2, conv_dw_w_2, conv_dw_b_2, conv_ln_g_2,
        conv_ln_b_2, w_out_2, ffn_norm_g_2, w_up_2, ffn_dw_w_2, ffn_dw_b_2, w_down_2,
    )


_drawn_inputs = setup_inputs


def setup_inputs(seed=0):
    import zlib

    import numpy as np

    out = dict(_drawn_inputs(seed))
    spreads = {}
    factors = {'gla_gate_b': 5.015,
     'gla_out_norm': 5.1,
     'mla_q_lora_norm': 8.0,
     'mla_kv_lora_norm': 8.0,
     'mla_q_norm': 8.0,
     'mla_k_norm': 8.0,
     'ffn_conv_b': 6.059,
     'mix_norm_g_2': 7.408,
     'mem_norm_g_2': 8.0,
     'q_norm_g_2': 8.0,
     'k_norm_g_2': 8.0,
     'mq_norm_g_2': 8.0,
     'mk_norm_g_2': 8.0,
     'conv_dw_b_2': 4.762,
     'conv_ln_g_2': 7.767,
     'conv_ln_b_2': 8.0,
     'ffn_norm_g_2': 3.95,
     'ffn_dw_b_2': 4.129}
    for name, (base, spread) in spreads.items():
        noise = np.random.default_rng([zlib.crc32(name.encode()), seed]).standard_normal(out[name].shape)
        drawn = base * np.exp(spread * noise) if base else spread * noise
        out[name] = __import__('jax').numpy.asarray(drawn.astype(out[name].dtype))
    for name, factor in factors.items():
        out[name] = (out[name] * factor).astype(out[name].dtype)
    return out
```

```python
from contextlib import ExitStack

import numpy as np

import concourse.bass as bass
from concourse import mybir

F32 = mybir.dt.float32
F32R = mybir.dt.float32r
I32 = mybir.dt.int32
U32 = mybir.dt.uint32
ACT = mybir.ActivationFunctionType
ALU = mybir.AluOpType
AX_X = mybir.AxisListType.X

P = 128
D = 1024
KD = D // P
T = 256
TT = 2 * T
EPS = 1e-6
RING = 4
FF_T = 2816 // P
CH = 64
NCH = TT // CH
GH, MH, AH, MEMH = 4, 8, 8, 4

STREAM = [("ada0", 48), ("gate", 1), ("gq", 4), ("gk", 4), ("gv", 8), ("gr", 8), ("go", 8),
          ("up0", 2 * FF_T), ("dn0", 24), ("ada1", 48),
          ("ckv", 2), ("kpe", 1), ("cq", 3), ("uq", 6), ("uk", 2), ("uv", 2), ("mo", 8),
          ("up1", 2 * FF_T), ("dn1", 24),
          ("sqk", 8), ("sv", 4), ("sglu", 4), ("sqm", 2), ("mk", 2), ("mv", 2), ("so", 8),
          ("up2", 2 * FF_T), ("dn2", 24)]
START = {}
NSLOTS = 0
for _name, _count in STREAM:
    START[_name] = NSLOTS
    NSLOTS += _count

PARAMS = [("c", 16), ("b_ada0", 96), ("b_ada1", 96), ("g_mix0", 16), ("g_mix1", 16), ("g_ffn0", 16), ("g_ffn1", 16),
          ("gate_b", 8), ("g_out", 2), ("g_ql", 3), ("g_kvl", 2), ("g_qn", 1), ("g_qr", 1), ("g_kn", 1), ("g_kr", 1)]
PARAMS += [(f"cw{f}_{t}", 44) for f in range(3) for t in range(3)] + [(f"cb{f}", 44) for f in range(3)]
PARAMS += [("g_smix", 8), ("g_mem", 8), ("g_sq", 1), ("g_sk", 1), ("g_smq", 1), ("g_smk", 1),
           ("dw", 62), ("dwb", 2), ("ln_g", 2), ("ln_b", 2), ("g_sffn", 8)]
NORMS = ["mix0", "ffn0", "mix1", "ffn1", "smix", "smem", "sffn"]
PCOL = {}
NPARAM = 0
for _name, _count in PARAMS:
    PCOL[_name] = NPARAM
    NPARAM += _count

CONSTS = [("ident", 128), ("ones", 128), ("blk64", 128), ("sel4", 2), ("invf", 1)]
CCOL = {}
NCONST = 0
for _name, _count in CONSTS:
    CCOL[_name] = NCONST
    NCONST += _count


def build(nc, wstream, params, consts, x_in, ctx_in, mem_in, pos_in, w2_in, gla_c, mla_c, sec_c, out):
    with ExitStack() as ctx:
        def sem(name):
            return ctx.enter_context(nc.semaphore(name))

        S = {}
        names = "xin ctxin parin constin w2in glac mlac secc memin posin outd csil c4 amod0 amod1"
        for L in (0, 1):
            names += f" ada{L}_rows ada{L}_tr ada{L}_out"
        names += " n_sq n_ss n_rv n_rstd n_xn n_h n_hi n_lo"
        for t in ("f0", "f1", "f2"):
            names += f" {t}_u {t}_c1 {t}_free {t}_s {t}_hf {t}_pair {t}_dn"
        names += " z1 gqk gvc g_z g_abs g_l g_zd g_b g_e g_q g_kt g_kst g_sc g_am g_U g_S g_o g_of g_osq g_oss g_orv g_orstd g_on g_sr g_y go_x"
        names += " m_dn m_csq m_css m_crv m_crstd m_cn m_clo m_kn m_qn m_v m_qsq m_qss m_qrv m_qrstd m_ksq m_kss m_krv m_krstd m_kn2 m_sw m_rot"
        names += " a_s a_max a_exp a_pn a_t a_pt a_o a_oh mo_x"
        names += " t_tab t_sin s_ev s_vc s_glu s_qsq s_qss s_qrv s_qrstd s_qn s_sw s_rot s_mu s_xc s_csq s_cvs s_crv s_crstd s_cn s_cs s_ch"
        names += " b_s b_sb b_max b_exp b_pn b_t b_pt b_o b_oh so_x dve_step act_step slot_used hi_ready lo_ready"
        for name in names.split():
            S[name] = sem(name)
        raw_in = [sem(f"raw_in{j}") for j in range(RING)]

        def sb(stack, name, shape, dt=F32):
            return stack.enter_context(nc.sbuf_tensor(name, shape, dt))

        XT = sb(ctx, "XT", [P, KD, TT])
        Hhi = sb(ctx, "Hhi", [P, KD, TT], F32R)
        Hlo = sb(ctx, "Hlo", [P, KD, TT], F32R)
        raw = sb(ctx, "raw", [P, RING, 1024])
        whi = sb(ctx, "whi", [P, RING, 1024], F32R)
        wlo = sb(ctx, "wlo", [P, RING, 1024], F32R)
        par = sb(ctx, "par", [P, NPARAM])
        con = sb(ctx, "con", [P, NCONST])
        c4 = sb(ctx, "c4", [P, KD, P], F32R)
        ada = [sb(ctx, f"ada{L}", [P, 96]) for L in (0, 1)]
        amod = [sb(ctx, f"amod{L}", [P, 32]) for L in (0, 1)]
        rstd = sb(ctx, "rstd", [P, TT])
        ps = ctx.enter_context(nc.psum_tensor("ps", [P, 8, 512], F32))

        with ExitStack() as part:
            Hf0 = sb(part, "Hf0", [P, KD, TT])
            gq = sb(part, "gq", [P, GH, TT])
            gk = sb(part, "gk", [P, GH, TT])
            gv = sb(part, "gv", [P, 4, D])
            glac = sb(part, "glac", [P, 2 * P + TT])
            w2 = sb(part, "w2", [P, TT])
            z1 = sb(part, "z1", [P, TT])
            glog = sb(part, "glog", [P, 2, TT])
            gcum = sb(part, "gcum", [P, 3, TT])
            gexp = sb(part, "gexp", [P, 3, TT])
            gtot = sb(part, "gtot", [P, 2, NCH])
            qdec = sb(part, "qdec", [P, 2, TT])
            kint = sb(part, "kint", [P, 2, TT])
            kstf = sb(part, "kstf", [P, 2, TT])
            kst = sb(part, "kst", [P, 4, P])
            am = sb(part, "am", [P, 2, TT])
            Sh = sb(part, "Sh", [P, NCH, 2 * P])
            row0 = Sh[:, :, :].rearrange("p (q a) b -> p q (a b)", q=2)
        with ExitStack() as part:
            of = sb(part, "of", [P, KD, TT])
            yhi = sb(part, "yhi", [P, KD, TT], F32R)
            ylo = sb(part, "ylo", [P, KD, TT], F32R)
            sb(part, "glac_", [P, 2 * P + TT])
            orstd = sb(part, "orstd", [P, GH, TT])
            osq = sb(part, "osq", [P, 2, TT])
            sr = sb(part, "sr", [P, 2, TT])
            yf = sb(part, "yf", [P, 2, TT])
        with ExitStack() as part:
            hidhi = sb(part, "hidhi", [P, FF_T, TT], F32R)
            hidlo = sb(part, "hidlo", [P, FF_T, TT], F32R)
            u = sb(part, "u", [P, 4, TT])
            sg = sb(part, "sg", [P, TT])
            hf = rstd
        with ExitStack() as part:
            Hff = sb(part, "Hff", [P, KD, TT])
        with ExitStack() as part:
            Hf1 = sb(part, "Hf1", [P, KD, TT])
            mlac = sb(part, "mlac", [P, P + 2 * T])
            cq = sb(part, "cq", [P, 3, T])
            ckv = sb(part, "ckv", [P, 2, TT])
            kpe = sb(part, "kpe", [P, TT])
            cqhi = sb(part, "cqhi", [P, 3, T], F32R)
            cqlo = sb(part, "cqlo", [P, 3, T], F32R)
            ckvhi = sb(part, "ckvhi", [P, 2, TT], F32R)
            ckvlo = sb(part, "ckvlo", [P, 2, TT], F32R)
            mq = sb(part, "mq", [P, 12, T])
            kn = sb(part, "kn", [P, MH, TT])
            adarow1 = kn[:, 0:4, :].rearrange("p (q a) t -> p q (a t)", q=2)
            mv = sb(part, "mv", [P, 4, D])
            gsc = sb(part, "gsc", [P, 2])
            mrq = sb(part, "mrq", [P, 6, TT])
            mrst = mrq[:, 3:6, :]
            amx = sb(part, "amx", [P, 2, 2])
            asum = sb(part, "asum", [P, 2, 2])
            arec = sb(part, "arec", [P, 2, 2])
        with ExitStack() as part:
            Pm = sb(part, "Pm", [P, 2, 2, TT])
            PTm = sb(part, "PTm", [P, 4, T])
        with ExitStack() as part:
            Hf2 = sb(part, "Hf2", [P, KD, T])
            memx = sb(part, "memx", [P, KD, T])
            memhi = sb(part, "memhi", [P, KD, T], F32R)
            memlo = sb(part, "memlo", [P, KD, T], F32R)
            secc = sb(part, "secc", [P, P + 2 * T])
            posi = sb(part, "posi", [P, T], I32)
            tab = sb(part, "tab", [P, 4, T])
            sq_ = sb(part, "sq_", [P, 12, T])
            sqs = sb(part, "sqs", [P, 12, T])
            svt = sb(part, "svt", [P, 2, TT])
            svm = sb(part, "svm", [P, 2, T])
            sga = sb(part, "sga", [P, 2, T])
            sgg = sb(part, "sgg", [P, 2, T])
            cpad = sb(part, "cpad", [P, 2, T + 30])
            cacc = sb(part, "cacc", [P, 2, T])
            csq = sb(part, "csq", [P, 2, T])
            crst = sb(part, "crst", [P, 3, T])
            gsc2 = sb(part, "gsc2", [P, 2])
            Sb = sb(part, "Sb", [P, 2, 2, T])
            Pb = sb(part, "Pb", [P, 2, 2, T])
            PTb = sb(part, "PTb", [P, 2, 2, T])
            bmx = sb(part, "bmx", [P, 2, 2])
            bsum = sb(part, "bsum", [P, 2, 2])
            brec = sb(part, "brec", [P, 2, 2])

        ident = con[:, CCOL["ident"]:CCOL["ident"] + P]
        ones = con[:, CCOL["ones"]:CCOL["ones"] + P]
        blk64 = con[:, CCOL["blk64"]:CCOL["blk64"] + P]

        def pc(name, j=0, n=1):
            return par[:, PCOL[name] + j:PCOL[name] + j + n]

        def pdyn(name, j):
            return par[:, bass.ds(PCOL[name] + j, 1)]

        def load_slot(sp, n, it=0):
            if n >= RING:
                sp.wait_ge(S["lo_ready"], n - RING + 1 + it)
            sp.dma_start(raw[:, n % RING, :], wstream[n + it]).then_inc(raw_in[n % RING], 16)

        def hi_slot(act, n, it=0):
            act.wait_ge(raw_in[n % RING], 16 * (n // RING + 1) + 4 * it)
            if n >= RING:
                act.wait_ge(S["slot_used"], n - RING + 1 + it)
            nc.scalar.activation(whi[:, n % RING, :], raw[:, n % RING, :], ACT.Copy).then_inc(S["hi_ready"], 1)

        def lo_slot(pool, n, it=0):
            pool.wait_ge(S["hi_ready"], n + 1 + it)
            if n >= RING:
                pool.wait_ge(S["slot_used"], n - RING + 1 + it)
            nc.gpsimd.tensor_tensor(wlo[:, n % RING, :], raw[:, n % RING, :], whi[:, n % RING, :].bitcast(F32),
                                    ALU.subtract).then_inc(S["lo_ready"], 1)

        def slot_products(pe, n, it, hi_products, lo_products):
            pe.wait_ge(S["hi_ready"], n + 1 + it)
            for source, products in ((whi, hi_products), (wlo, lo_products)):
                if source is wlo:
                    pe.wait_ge(S["lo_ready"], n + 1 + it)
                for o, c0, width, stationary, other, start, stop in products:
                    w = source[:, n % RING, c0:c0 + width]
                    a, b = (w, other) if stationary else (other, w)
                    mm = nc.tensor.matmul(o, a, b, start=start, stop=stop)
            mm.then_inc(S["slot_used"], 1)

        def tile_products(pe, n, it, o, c0, k0, kn_, xhi, xlo, start, stop):
            his, los = [], []
            for k in range(kn_):
                c = c0 + k * P
                his.append((o, c, P, True, xhi(k0 + k), start and k == 0, False))
                his.append((o, c, P, True, xlo(k0 + k), False, False))
                los.append((o, c, P, True, xhi(k0 + k), False, stop and k == kn_ - 1))
            return his, los

        def H(t0, n):
            return (lambda k: Hhi[:, k, t0:t0 + n]), (lambda k: Hlo[:, k, t0:t0 + n])

        def column_tile(pe, n, bank, xhi, xlo, ntok, it=0):
            his, los = tile_products(pe, n, it, ps[:, bank, 0:ntok], 0, 0, KD, xhi, xlo, True, True)
            slot_products(pe, n, it, his, los)

        def normed(t):
            return S["n_lo"], KD * (NORMS.index(t) + 1)

        block = ctx.enter_context(nc.Block())

        counters = {"d": 0, "a": 0}

        def dlink(ins):
            counters["d"] += 1
            ins.then_inc(S["dve_step"], 1)
            nc.vector.wait_ge(S["dve_step"], counters["d"])

        def alink(ins):
            counters["a"] += 1
            ins.then_inc(S["act_step"], 1)
            nc.scalar.wait_ge(S["act_step"], counters["a"])

        def ada_pe(pe, L, row):
            s0 = START[f"ada{L}"]
            pe.wait_ge(S["c4"], 2)
            with pe.Fori(0, 3) as i:
                it = i * 16
                for q in range(2):
                    for k in range(KD):
                        prods = [(ps[:, 2 * q + h, :], h * 512, 512, False, c4[:, k, :]) for h in range(2)]
                        slot_products(pe, s0 + q * 8 + k, it, [(*x, k == 0, False) for x in prods],
                                      [(*x, False, k == KD - 1) for x in prods])
                for q in range(2):
                    pe.wait_ge(S[f"ada{L}_rows"], i * 2 + q + 1)
                    for j in range(KD):
                        mm = nc.tensor.matmul(ps[:, 4 + q, 2 * j:2 * j + 2], row[0:4, q, j * P:(j + 1) * P],
                                              con[0:4, CCOL["sel4"]:CCOL["sel4"] + 2], start=True, stop=True)
                    mm.then_inc(S[f"ada{L}_tr"], 1)

        def ada_act(act, L):
            s0 = START[f"ada{L}"]
            with act.Fori(0, 3) as i:
                for j in range(16):
                    hi_slot(act, s0 + RING + j, i * 16)

        def ada_dve(dve, L, row):
            s0 = START[f"ada{L}"]
            with dve.Fori(0, 3) as i:
                for q in range(2):
                    dve.wait_ge(S["slot_used"], i * 16 + s0 + 8 * (q + 1))
                    nc.vector.tensor_copy(row[0:4, q, :], ps[0:4, 2 * q:2 * q + 2, :].rearrange("p a b -> p (a b)")).then_inc(S[f"ada{L}_rows"], 1)
                for q in range(2):
                    dve.wait_ge(S[f"ada{L}_tr"], i * 2 + q + 1)
                    col = PCOL[f"b_ada{L}"] + 16 * q
                    nc.vector.tensor_tensor(ada[L][:, bass.ds(i * 32 + 16 * q, 16)], ps[:, 4 + q, 0:16],
                                            par[:, bass.ds(i * 32 + col, 16)], ALU.add).then_inc(S[f"ada{L}_out"], 1)
            dve.wait_ge(S[f"ada{L}_out"], 6)
            for n, (part_, g) in enumerate(((1, f"g_mix{L}"), (4, f"g_ffn{L}"))):
                nc.vector.scalar_tensor_tensor(amod[L][:, 16 * n:16 * n + 16], ada[L][:, 16 * part_:16 * part_ + 16], 1.0,
                                               pc(g, 0, 16), ALU.add, ALU.mult).then_inc(S[f"amod{L}"], 1)

        def norm_act(act, t, src, ready, ntok, scale, shift, Hf):
            for k in range(KD):
                for s, v in ready(k):
                    act.wait_ge(s, v)
                nc.scalar.activation(Hf[:, k, 0:ntok], src(k), ACT.Square).then_inc(S["n_sq"], 1)
            act.wait_ge(S["n_rv"], NORMS.index(t) + 1)
            nc.scalar.activation(rstd[:, 0:ntok], rstd[:, 0:ntok], ACT.Sqrt).then_inc(S["n_rstd"], 1)
            for k in range(KD):
                act.wait_ge(S["n_xn"], KD * NORMS.index(t) + k + 1)
                for h in range(ntok // T):
                    seg = Hf[:, k, h * T:(h + 1) * T]
                    if shift is None:
                        mm = nc.scalar.activation(seg, seg, ACT.Copy, scale=scale(k, h))
                    else:
                        mm = nc.scalar.activation(seg, seg, ACT.Identity, scale=scale(k, h), bias=shift(k, h))
                mm.then_inc(S["n_h"], 1)

        def norm_pe(pe, t, ntok, Hf):
            for k in range(KD):
                pe.wait_ge(S["n_sq"], KD * NORMS.index(t) + k + 1)
                mm = nc.tensor.matmul(ps[:, 7, 0:ntok], ones, Hf[:, k, 0:ntok], start=k == 0, stop=k == KD - 1)
            mm.then_inc(S["n_ss"], 1)

        def norm_dve(dve, t, src, ntok, Hf, hi, lo):
            dve.wait_ge(S["n_ss"], NORMS.index(t) + 1)
            dlink(nc.vector.tensor_scalar(rstd[:, 0:ntok], ps[:, 7, 0:ntok], 1.0 / D, EPS, ALU.mult, ALU.add))
            nc.vector.reciprocal(rstd[:, 0:ntok], rstd[:, 0:ntok]).then_inc(S["n_rv"], 1)
            dve.wait_ge(S["n_rstd"], NORMS.index(t) + 1)
            for k in range(KD):
                nc.vector.tensor_tensor(Hf[:, k, 0:ntok], src(k), rstd[:, 0:ntok], ALU.mult).then_inc(S["n_xn"], 1)
            for k in range(KD):
                dve.wait_ge(S["n_h"], KD * NORMS.index(t) + k + 1)
                nc.vector.tensor_copy(hi(k), Hf[:, k, 0:ntok]).then_inc(S["n_hi"], 1)
                dve.wait_ge(S["n_hi"], KD * NORMS.index(t) + k + 1)
                nc.vector.tensor_tensor(lo(k), Hf[:, k, 0:ntok], hi(k).bitcast(F32), ALU.subtract).then_inc(S["n_lo"], 1)

        def ffn_pe(pe, f, ntok):
            s0, t = START[f"up{f}"], f"f{f}"
            xhi, xlo = H(0, TT) if ntok == TT else H(T, T)
            with pe.Fori(0, FF_T // 2) as i:
                for j in range(4):
                    pe.wait_ge(S[f"{t}_free"], i * 4 + j + 1)
                    column_tile(pe, s0 + j, j, xhi, xlo, ntok, i * 4)
            d0 = START[f"dn{f}"]
            with pe.Fori(0, 2) as i:
                for m in range(4):
                    pe.wait_ge(S[f"{t}_dn"], i * 4 + m + 1)
                    for part_, (k0, kn_) in enumerate(((0, 8), (8, 8), (16, 6))):
                        pe.wait_ge(S[f"{t}_pair"], 2 + k0 + kn_)
                        his, los = tile_products(pe, 0, 0, ps[:, 4 + m, 0:ntok], 0, k0, kn_,
                                                 lambda k: hidhi[:, k, 0:ntok], lambda k: hidlo[:, k, 0:ntok],
                                                 part_ == 0, part_ == 2)
                        slot_products(pe, d0 + 3 * m + part_, i * 12, his, los)

        def ffn_act(act, f, ntok):
            s0, t = START[f"up{f}"], f"f{f}"
            with act.Fori(0, FF_T // 2) as i:
                for pair in range(2):
                    act.wait_ge(S[f"{t}_pair"], i * 2 + pair + 1)
                    for ab in range(2):
                        j = 2 * pair + ab
                        act.wait_ge(S["slot_used"], i * 4 + s0 + j + 1)
                        nc.scalar.activation(u[:, j, 0:ntok], ps[:, j, 0:ntok], ACT.Identity,
                                             scale=pdyn(f"cw{f}_1", i * 4 + j), bias=pdyn(f"cb{f}", i * 4 + j)).then_inc(S[f"{t}_u"], 1)
                        hi_slot(act, s0 + RING + j, i * 4)
                    act.wait_ge(S[f"{t}_free"], i * 4 + 4 + 2 * pair + 2)
                    nc.scalar.activation(sg[:, 0:ntok], u[:, 2 * pair + 1, 0:ntok], ACT.Silu).then_inc(S[f"{t}_s"], 1)
            d0 = START[f"dn{f}"]
            if f < 2:
                with act.Fori(0, 2) as i:
                    for j in range(12):
                        hi_slot(act, d0 + RING + j, i * 12)
            else:
                for j in range(24 - RING):
                    hi_slot(act, d0 + RING + j)

        def ffn_dve(dve, f, ntok, gate):
            t = f"f{f}"
            for _ in range(4):
                dve.sem_inc(S[f"{t}_free"], 1)
                dve.sem_inc(S[f"{t}_dn"], 1)
            for _ in range(2):
                dve.sem_inc(S[f"{t}_pair"], 1)

            def seg(ap, a, b):
                return ap[:, 0:ntok].rearrange("p (s t) -> p s t", t=T)[:, :, a:b]
            with dve.Fori(0, FF_T // 2) as i:
                for pair in range(2):
                    for j in (2 * pair, 2 * pair + 1):
                        dve.wait_ge(S[f"{t}_u"], i * 4 + j + 1)
                        acc, tile = u[:, j, :], ps[:, j, :]
                        nc.vector.scalar_tensor_tensor(seg(acc, 1, T), seg(tile, 0, T - 1), pdyn(f"cw{f}_0", i * 4 + j), seg(acc, 1, T),
                                                       ALU.mult, ALU.add).then_inc(S[f"{t}_c1"], 1)
                        dve.wait_ge(S[f"{t}_c1"], i * 4 + j + 1)
                        nc.vector.scalar_tensor_tensor(seg(acc, 0, T - 1), seg(tile, 1, T), pdyn(f"cw{f}_2", i * 4 + j), seg(acc, 0, T - 1),
                                                       ALU.mult, ALU.add).then_inc(S[f"{t}_free"], 1)
                    dve.wait_ge(S[f"{t}_free"], i * 4 + 4 + 2 * pair + 2)
                    dve.wait_ge(S[f"{t}_s"], i * 2 + pair + 1)
                    k = i * 2 + pair
                    nc.vector.tensor_tensor(hf[:, 0:ntok], sg[:, 0:ntok], u[:, 2 * pair, 0:ntok], ALU.mult).then_inc(S[f"{t}_hf"], 1)
                    dve.wait_ge(S[f"{t}_hf"], i * 4 + 2 * pair + 1)
                    nc.vector.tensor_copy(hidhi[:, k, 0:ntok], hf[:, 0:ntok]).then_inc(S[f"{t}_hf"], 1)
                    dve.wait_ge(S[f"{t}_hf"], i * 4 + 2 * pair + 2)
                    nc.vector.tensor_tensor(hidlo[:, k, 0:ntok], hf[:, 0:ntok], hidhi[:, k, 0:ntok].bitcast(F32),
                                            ALU.subtract).then_inc(S[f"{t}_pair"], 1)
            d0 = START[f"dn{f}"]
            with dve.Fori(0, 2) as i:
                for m in range(4):
                    dve.wait_ge(S["slot_used"], i * 12 + d0 + 3 * m + 3)
                    add_residual(i * 4 + m, 4 + m, ntok, gate, S[f"{t}_dn"])

        def add_residual(m, bank, ntok, gate, signal):
            for h in range(2 - ntok // T, 2):
                x = XT[:, m, h * T:(h + 1) * T]
                y = ps[:, bank, (h * T if ntok == TT else 0):(h * T if ntok == TT else 0) + T]
                if gate is None:
                    ins = nc.vector.tensor_tensor(x, y, x, ALU.add)
                else:
                    L, part_ = gate
                    ins = nc.vector.scalar_tensor_tensor(x, y, ada[L][:, bass.ds(m * 2 + 16 * part_ + h, 1)], x, ALU.mult, ALU.add)
            ins.then_inc(signal, 1)

        def out_pe(pe, stage, xhi, xlo, ntok, signal, split_ready):
            s0 = START[stage]
            for s, v in split_ready:
                pe.wait_ge(s, v)
            with pe.Fori(0, 2) as i:
                for j in range(4):
                    pe.wait_ge(signal, i * 4 + j + 1)
                    column_tile(pe, s0 + j, j, xhi, xlo, ntok, i * 4)

        def out_act(act, stage):
            s0 = START[stage]
            with act.Fori(0, 2) as i:
                for j in range(4):
                    hi_slot(act, s0 + RING + j, i * 4)

        def out_dve(dve, stage, ntok, gate, signal):
            s0 = START[stage]
            for _ in range(4):
                dve.sem_inc(signal, 1)
            with dve.Fori(0, 2) as i:
                for j in range(4):
                    dve.wait_ge(S["slot_used"], i * 4 + s0 + j + 1)
                    add_residual(i * 4 + j, j, ntok, gate, signal)

        ORDER = [[0, 1, 2, 3, 4, 5, 6, 7], [3, 2, 1, 0, 7, 6, 5, 4]]
        OBANK = (4, 6)

        def update(ch):
            return ps[:, 2 * (ch % 2) + ch // 4, 256 * (ch // 2 % 2):256 * (ch // 2 % 2) + 256]

        def gla_pe(pe):
            xhi, xlo = H(0, TT)
            pe.wait_ge(*normed("mix0"))
            n = START["gate"]
            column_tile(pe, n, n % 4, xhi, xlo, TT)
            for m in range(8):
                n = START["gq"] + m
                if m >= 3:
                    pe.wait_ge(S["gqk"], m - 3) if m > 3 else pe.wait_ge(S["z1"], 1)
                column_tile(pe, n, n % 4, xhi, xlo, TT)
            for c in range(2):
                banks = [4, 5, 6, 7] if c == 0 else [0, 1, 2, 3]
                if c == 1:
                    pe.wait_ge(S["gqk"], 8)
                for kp in range(4):
                    n = START["gv"] + 4 * c + kp
                    his, los = [], []
                    for k2 in range(2):
                        k = 2 * kp + k2
                        for tt in range(4):
                            o = ps[:, banks[tt], :]
                            a, b = Hhi[:, k, tt * P:(tt + 1) * P], Hlo[:, k, tt * P:(tt + 1) * P]
                            his.append((o, k2 * 512, 512, False, a, k == 0, False))
                            his.append((o, k2 * 512, 512, False, b, False, False))
                            los.append((o, k2 * 512, 512, False, a, False, k == KD - 1))
                    slot_products(pe, n, 0, his, los)
            pe.wait_ge(S["w2in"], 16)
            pe.wait_ge(S["gvc"], 8)

            def z(c):
                h, d = divmod(c, 2)
                if c >= 1:
                    pe.wait_ge(S["g_abs"], c)
                    pe.wait_ge(S["g_zd"], c)
                nc.tensor.matmul(ps[:, 7, :], w2[32 * d:32 * d + 16, h * P:(h + 1) * P], z1[32 * d:32 * d + 16, :],
                                 start=True, stop=True).then_inc(S["g_z"], 1)
            z(0)
            for c in range(2 * GH):
                h, d = divmod(c, 2)
                if c + 1 < 2 * GH:
                    z(c + 1)
                b = c % 2
                pe.wait_ge(S["g_q"], 3 * c + 3)
                if c >= 1:
                    pe.wait_ge(S["g_S"], 7 * c)
                for tt in range(4):
                    mm = nc.tensor.transpose(ps[:, 0, tt * P:(tt + 1) * P], kstf[:, b, tt * P:(tt + 1) * P], ident)
                mm.then_inc(S["g_kt"], 1)
                if c >= 1:
                    pe.wait_ge(S["g_am"], c)
                for tt in range(4):
                    sl = slice(tt * P, (tt + 1) * P)
                    mm = nc.tensor.matmul(ps[:, 5, sl], kint[:, b, sl], qdec[:, b, sl], start=True, stop=True)
                mm.then_inc(S["g_sc"], 1)
                pe.wait_ge(S["g_kst"], c + 1)
                for j in range(NCH - 1):
                    ch = ORDER[d][j]
                    p0 = CH * (ch % 2)
                    mm = nc.tensor.matmul(update(ch), kst[p0:p0 + CH, ch // 2, :],
                                          gv[p0:p0 + CH, ch // 2, h * 256:(h + 1) * 256], start=True, stop=True)
                mm.then_inc(S["g_U"], 1)
                pe.wait_ge(S["g_am"], c + 1)
                if d == 0 and h >= 1:
                    pe.wait_ge(S["g_of"], h)
                for vt in range(2):
                    for tt in range(4):
                        nc.tensor.matmul(ps[:, OBANK[vt], tt * P:(tt + 1) * P], gv[:, tt, h * 256 + vt * P:h * 256 + (vt + 1) * P],
                                         am[:, d, tt * P:(tt + 1) * P], start=(d == 0 and tt == 0), stop=False, skip_group_check=True)
                for j in range(1, NCH):
                    ch = ORDER[d][j]
                    pe.wait_ge(S["g_S"], 7 * c + j)
                    for vt in range(2):
                        mm = nc.tensor.matmul(ps[:, OBANK[vt], ch * CH:(ch + 1) * CH], Sh[:, j, vt * P:(vt + 1) * P],
                                              qdec[:, b, ch * CH:(ch + 1) * CH], start=False, stop=(d == 1 and j == NCH - 1), skip_group_check=True)
                mm.then_inc(S["g_o"], 1)
            for h in range(GH):
                pe.wait_ge(S["g_osq"], 2 * h + 2)
                for vt in range(2):
                    mm = nc.tensor.matmul(ps[:, h, :], ones, osq[:, vt, :], start=vt == 0, stop=vt == 1)
                mm.then_inc(S["g_oss"], 1)
            for m in range(8):
                n = START["gr"] + m
                if m >= 4:
                    pe.wait_ge(S["g_sr"], m - 3)
                column_tile(pe, n, 4 + m % 4, xhi, xlo, TT)
            out_pe(pe, "go", lambda k: yhi[:, k, :], lambda k: ylo[:, k, :], TT, S["go_x"], [(S["g_y"], 16)])

        def gla_act(act):
            n = START["gate"]
            act.wait_ge(S["slot_used"], n + 1)
            nc.scalar.activation(z1[0:64, :], ps[0:64, n % 4, :], ACT.Copy).then_inc(S["z1"], 1)
            hi_slot(act, n + RING)
            for m in range(8):
                n = START["gq"] + m
                act.wait_ge(S["slot_used"], n + 1)
                dst = gq[:, m, :] if m < 4 else gk[:, m - 4, :]
                nc.scalar.activation(dst, ps[:, n % 4, :], ACT.Copy, scale=float(P) ** -0.5 if m < 4 else 1.0).then_inc(S["gqk"], 1)
                hi_slot(act, n + RING)
            for j in range(8):
                hi_slot(act, START["gv"] + j + RING)

            def logs(c):
                act.wait_ge(S["g_z"], c + 1)
                if c >= 1:
                    act.wait_ge(S["g_b"], c)
                l = glog[:, 0, :]
                nc.scalar.activation(l, ps[:, 7, :], ACT.Abs, bias=pc("gate_b", c)).then_inc(S["g_abs"], 1)
                act.wait_ge(S["g_abs"], c + 1)
                alink(nc.scalar.activation(l, l, ACT.Exp, scale=-1.0))
                nc.scalar.activation(l, l, ACT.Ln, bias=1.0).then_inc(S["g_l"], 1)

            def exps(c):
                act.wait_ge(S["g_b"], c + 1)
                if c >= 1:
                    act.wait_ge(S["g_q"], 3 * c)
                if c >= 2:
                    act.wait_ge(S["g_S"], 7 * (c - 1))
                rc = gcum[:, 1, :] if c % 2 else gcum[:, 0, :]
                tot = gcum[:, 0, :].rearrange("p (c t) -> p c t", t=CH)[:, :, CH - 1]
                nc.scalar.activation(gexp[:, 2, :], gcum[:, 2, :], ACT.Exp, scale=1 / 16).then_inc(S["g_e"], 1)
                nc.scalar.activation(gexp[:, 0, :], rc, ACT.Exp, scale=1 / 16).then_inc(S["g_e"], 1)
                nc.scalar.activation(gexp[:, 1, :], rc, ACT.Exp, scale=-1 / 16).then_inc(S["g_e"], 1)
                nc.scalar.activation(gtot[:, c % 2, :], tot, ACT.Exp, scale=1 / 16).then_inc(S["g_e"], 1)

            def after(c):
                act.wait_ge(S["g_kt"], c + 1)
                if c >= 1:
                    act.wait_ge(S["g_U"], c)
                nc.scalar.activation(kst[:, :, :], ps[:, 0, :].rearrange("p (a b) -> p a b", b=P), ACT.Copy).then_inc(S["g_kst"], 1)

            logs(0)
            exps(0)
            for c in range(2 * GH):
                if c + 1 < 2 * GH:
                    logs(c + 1)
                after(c)
                if c + 1 < 2 * GH:
                    exps(c + 1)
                if c % 2:
                    act.wait_ge(S["g_o"], c + 1)
                    h = c // 2
                    for vt in range(2):
                        ins = nc.scalar.activation(of[:, 2 * h + vt, :], ps[:, OBANK[vt], :], ACT.Copy)
                    ins.then_inc(S["g_of"], 1)
            for h in range(GH):
                act.wait_ge(S["g_of"], h + 1)
                if h >= 1:
                    act.wait_ge(S["g_oss"], h)
                for vt in range(2):
                    nc.scalar.activation(osq[:, vt, :], of[:, 2 * h + vt, :], ACT.Square).then_inc(S["g_osq"], 1)
            act.wait_ge(S["g_orv"], 1)
            nc.scalar.activation(orstd[:, :, :], orstd[:, :, :], ACT.Sqrt).then_inc(S["g_orstd"], 1)
            for m in range(8):
                n = START["gr"] + m
                act.wait_ge(S["slot_used"], n + 1)
                if m >= 2:
                    act.wait_ge(S["g_y"], 2 * (m - 1))
                nc.scalar.activation(sr[:, m % 2, :], ps[:, 4 + m % 4, :], ACT.Silu).then_inc(S["g_sr"], 1)
                hi_slot(act, n + RING)
            out_act(act, "go")

        def gla_dve(dve):
            for c in range(2):
                for tt in range(4):
                    if tt == 0:
                        dve.wait_ge(S["slot_used"], START["gv"] + 4 * c + 4)
                    nc.vector.tensor_copy(gv[:, tt, c * 512:(c + 1) * 512], ps[:, (4 if c == 0 else 0) + tt, :]).then_inc(S["gvc"], 1)
            dlink(nc.vector.memset(am[:, :, :], 0.0))
            dve.wait_ge(S["glac"], 16)
            dve.wait_ge(S["gqk"], 8)

            def first(c):
                h, d = divmod(c, 2)
                b = c % 2
                G, cs, rc, tb = glog[:, 1, :], gcum[:, 0, :], gcum[:, 1, :], gcum[:, 2, :]
                dve.wait_ge(S["g_abs"], c + 1)
                nc.vector.tensor_scalar(G, ps[:, 7, :], pc("gate_b", c), 0.0, ALU.add, ALU.min).then_inc(S["g_zd"], 1)
                dve.wait_ge(S["g_zd"], c + 1)
                dve.wait_ge(S["g_l"], c + 1)
                dlink(nc.vector.tensor_tensor(G, G, glog[:, 0, :], ALU.subtract))
                if c >= 1:
                    dve.wait_ge(S["g_e"], 4 * c)
                dlink(nc.vector.tensor_tensor_scan(cs, glac[:, 2 * P:2 * P + TT], G, 0.0, ALU.mult, ALU.add))
                c3 = cs.rearrange("p (c t) -> p c t", t=CH)
                tot = c3[:, :, CH - 1:CH].to_broadcast([P, NCH, CH])
                if d == 0:
                    nc.vector.tensor_tensor(tb.rearrange("p (c t) -> p c t", t=CH), tot, c3, ALU.subtract).then_inc(S["g_b"], 1)
                else:
                    dlink(nc.vector.tensor_tensor(tb, cs, G, ALU.subtract))
                    nc.vector.tensor_tensor(rc.rearrange("p (c t) -> p c t", t=CH), tot, tb.rearrange("p (c t) -> p c t", t=CH),
                                            ALU.subtract).then_inc(S["g_b"], 1)

            def second(c):
                h, b = c // 2, c % 2
                for n, (dst, src, e) in enumerate(((kstf, gk, 2), (qdec, gq, 0), (kint, gk, 1))):
                    dve.wait_ge(S["g_e"], 4 * c + n + 1)
                    if c >= 2 and n == 0:
                        dve.wait_ge(S["g_o"], c - 1)
                    nc.vector.tensor_tensor(dst[:, b, :], src[:, h, :], gexp[:, e, :], ALU.mult).then_inc(S["g_q"], 1)

            def third(c):
                d = c % 2
                dve.wait_ge(S["g_sc"], c + 1)
                if c >= 2:
                    dve.wait_ge(S["g_o"], c - 1)
                nc.vector.copy_predicated(am[:, d, :].rearrange("p (a t) -> p a t", t=P),
                                          glac[:, d * P:(d + 1) * P].bitcast(U32).rearrange("p (a t) -> p a t", a=1).to_broadcast([P, 4, P]),
                                          ps[:, 5, :].rearrange("p (a t) -> p a t", t=P)).then_inc(S["g_am"], 1)
                dve.wait_ge(S["g_U"], c + 1)
                dve.wait_ge(S["g_e"], 4 * c + 4)
                if c >= 1:
                    dve.wait_ge(S["g_o"], c)
                for j in range(NCH - 1):
                    ch = ORDER[d][j]
                    upd = update(ch)
                    if j == 0:
                        ins = nc.vector.tensor_copy(Sh[:, 1, :], upd)
                    else:
                        ins = nc.vector.scalar_tensor_tensor(Sh[:, j + 1, :], Sh[:, j, :], gtot[:, c % 2, ch:ch + 1], upd, ALU.mult, ALU.add)
                    ins.then_inc(S["g_S"], 1)
                    dve.wait_ge(S["g_S"], 7 * c + j + 1)

            first(0)
            second(0)
            for c in range(2 * GH):
                if c + 1 < 2 * GH:
                    first(c + 1)
                third(c)
                if c + 1 < 2 * GH:
                    second(c + 1)
            dve.wait_ge(S["g_oss"], GH)
            dlink(nc.vector.tensor_scalar(orstd[:, :, :], ps[:, 0:GH, :], 1.0 / 256, EPS, ALU.mult, ALU.add))
            nc.vector.reciprocal(orstd[:, :, :], orstd[:, :, :]).then_inc(S["g_orv"], 1)
            dve.wait_ge(S["g_orstd"], 1)
            for m in range(8):
                nc.vector.tensor_tensor(of[:, m, :], of[:, m, :], orstd[:, m // 2, :], ALU.mult).then_inc(S["g_on"], 1)
            for m in range(8):
                dve.wait_ge(S["g_on"], m + 1)
                dve.wait_ge(S["g_sr"], m + 1)
                dlink(nc.vector.scalar_tensor_tensor(yf[:, m % 2, :], of[:, m, :], pc("g_out", m % 2), sr[:, m % 2, :], ALU.mult, ALU.mult))
                nc.vector.tensor_copy(yhi[:, m, :], yf[:, m % 2, :]).then_inc(S["g_y"], 1)
                dve.wait_ge(S["g_y"], 2 * m + 1)
                nc.vector.tensor_tensor(ylo[:, m, :], yf[:, m % 2, :], yhi[:, m, :].bitcast(F32), ALU.subtract).then_inc(S["g_y"], 1)
            out_dve(dve, "go", TT, (0, 2), S["go_x"])

        MLA_SRC = [("ckv", 0, TT), ("ckv", 1, TT), ("kpe", 0, TT), ("cq", 0, T), ("cq", 1, T), ("cq", 2, T)]

        def mla_dst(n):
            name, j, ntok = MLA_SRC[n]
            return kpe[:, :] if name == "kpe" else (ckv if name == "ckv" else cq)[:, j, :]

        def mla_pe(pe):
            pe.wait_ge(*normed("mix1"))
            for m, (name, j, ntok) in enumerate(MLA_SRC):
                xhi, xlo = H(TT - ntok, ntok)
                if m >= 4:
                    pe.wait_ge(S["m_dn"], m - 3)
                column_tile(pe, START["ckv"] + m, m % 4, xhi, xlo, ntok)
            for bank, m0, cnt, lhs, ntok in ((4, 0, 2, ones, TT), (5, 2, 1, blk64, TT), (6, 3, 3, ones, T)):
                for j in range(cnt):
                    pe.wait_ge(S["m_csq"], m0 + j + 1)
                    mm = nc.tensor.matmul(ps[:, bank, 0:ntok], lhs, Hf1[:, m0 + j, 0:ntok], start=j == 0, stop=j == cnt - 1)
                mm.then_inc(S["m_css"], 1)
            pe.wait_ge(S["m_clo"], 5)
            pe.wait_ge(S["m_dn"], 6)
            for j in range(6):
                if j >= 2:
                    pe.wait_ge(S["m_qn"], j - 1)
                his, los = [], []
                for t2 in range(2):
                    a, b = tile_products(pe, 0, 0, ps[:, 2 * (j % 2) + t2, 0:T], t2 * 3 * P, 0, 3,
                                         lambda k: cqhi[:, k, :], lambda k: cqlo[:, k, :], True, True)
                    his += a
                    los += b
                slot_products(pe, START["uq"] + j, 0, his, los)
            pe.wait_ge(S["m_crv"], 3)
            for j in range(2):
                if j == 1:
                    pe.wait_ge(S["m_qn"], 6)
                his, los = [], []
                for t4 in range(4):
                    a, b = tile_products(pe, 0, 0, ps[:, (4 if j == 0 else 0) + t4, :], t4 * 2 * P, 0, 2,
                                         lambda k: ckvhi[:, k, :], lambda k: ckvlo[:, k, :], True, True)
                    his += a
                    los += b
                slot_products(pe, START["uk"] + j, 0, his, los)
            for j in range(2):
                pe.wait_ge(S["m_kn"], j + 1)
                his, los = [], []
                for k in range(2):
                    for tt in range(4):
                        o = ps[:, (4 if j == 0 else 0) + tt, :]
                        a, b = ckvhi[:, k, tt * P:(tt + 1) * P], ckvlo[:, k, tt * P:(tt + 1) * P]
                        his.append((o, k * 512, 512, False, a, k == 0, False))
                        his.append((o, k * 512, 512, False, b, False, False))
                        los.append((o, k * 512, 512, False, a, False, k == 1))
                slot_products(pe, START["uv"] + j, 0, his, los)
            pe.wait_ge(S["m_v"], 2)
            for j in range(6):
                pe.wait_ge(S["m_qsq"], 1 if j < 4 else 2)
                nc.tensor.matmul(ps[:, j, :], ones if j < 4 else blk64, Hf1[:, j, :], start=True, stop=True).then_inc(S["m_qss"], 1)
            pe.wait_ge(S["m_qrv"], 1)
            pe.wait_ge(S["m_ksq"], 1)
            for j in range(8):
                nc.tensor.matmul(ps[:, j, :], ones, Hf1[:, j, :], start=True, stop=True).then_inc(S["m_kss"], 1)
            pe.wait_ge(S["m_krv"], 1)
            pe.wait_ge(S["mlac"], 16)
            for j, x in enumerate((mq[:, 8:10, :], mq[:, 10:12, :], kpe[:, T:TT])):
                nc.tensor.matmul(ps[:, 5 + j, 0:T if j == 2 else TT], mlac[:, 0:P], x, start=True, stop=True).then_inc(S["m_sw"], 1)

            def scores(h):
                r0 = 64 * (h % 2)
                for qt in range(2):
                    bank = 2 * (h % 2) + qt
                    if h >= 2:
                        pe.wait_ge(S["a_exp"], 2 * (h - 2) + qt + 1)
                    qs = slice(qt * P, (qt + 1) * P)
                    nc.tensor.matmul(ps[:, bank, :], mq[:, h, qs], kn[:, h, :], start=True, stop=False)
                    nc.tensor.matmul(ps[:, bank, :], mq[r0:r0 + 64, 8 + h // 2, qs], kpe[r0:r0 + 64, :],
                                     start=False, stop=True).then_inc(S["a_s"], 1)
            pe.wait_ge(S["m_kn2"], 1)
            pe.wait_ge(S["m_rot"], 2)
            scores(0)
            for h in range(MH):
                if h + 1 < MH:
                    scores(h + 1)
                for qt in range(2):
                    pe.wait_ge(S["a_pn"], 2 * h + qt + 1)
                    if h >= 1:
                        pe.wait_ge(S["a_pt"], 2 * (h - 1) + qt + 1)
                    for kt in range(4):
                        mm = nc.tensor.transpose(ps[:, 4 + qt, kt * P:(kt + 1) * P], Pm[:, h % 2, qt, kt * P:(kt + 1) * P], ident)
                    mm.then_inc(S["a_t"], 1)
                pe.wait_ge(S["a_pt"], 2 * h + 2)
                if h >= 2:
                    pe.wait_ge(S["a_oh"], 2 * (h - 1))
                for kt in range(4):
                    mm = nc.tensor.matmul(ps[:, 6 + h % 2, 0:T], mv[:, kt, h * P:(h + 1) * P], PTm[:, kt, :], start=kt == 0, stop=kt == 3)
                mm.then_inc(S["a_o"], 1)
            out_pe(pe, "mo", lambda k: Hhi[:, k, 0:T], lambda k: Hlo[:, k, 0:T], T, S["mo_x"], [(S["a_oh"], 16)])

        def mla_act(act):
            for m, (name, j, ntok) in enumerate(MLA_SRC):
                n = START["ckv"] + m
                act.wait_ge(S["slot_used"], n + 1)
                nc.scalar.activation(mla_dst(m), ps[:, m % 4, 0:ntok], ACT.Copy).then_inc(S["m_dn"], 1)
                act.wait_ge(S["m_dn"], m + 1)
                if m == 0:
                    act.wait_ge(*normed("mix1"))
                nc.scalar.activation(Hf1[:, m, 0:ntok], mla_dst(m), ACT.Square).then_inc(S["m_csq"], 1)
                hi_slot(act, n + RING)
            for j, ntok in ((0, TT), (1, TT), (2, T)):
                act.wait_ge(S["m_crv"], j + 1)
                nc.scalar.activation(mrst[:, j, 0:ntok], mrst[:, j, 0:ntok], ACT.Sqrt).then_inc(S["m_crstd"], 1)
            for j in range(6):
                n = START["uq"] + j
                act.wait_ge(S["slot_used"], n + 1)
                b = 2 * (j % 2)
                nc.scalar.activation(mq[:, 2 * j:2 * j + 2, :], ps[:, b:b + 2, 0:T], ACT.Copy).then_inc(S["m_qn"], 1)
                hi_slot(act, n + RING)
            for j in range(2):
                n = START["uk"] + j
                act.wait_ge(S["slot_used"], n + 1)
                b = 4 if j == 0 else 0
                nc.scalar.activation(kn[:, 4 * j:4 * j + 4, :], ps[:, b:b + 4, :], ACT.Copy).then_inc(S["m_kn"], 1)
                hi_slot(act, n + RING)
            for j in range(2):
                hi_slot(act, START["uv"] + j + RING)
            act.wait_ge(S["m_css"], 3)
            act.wait_ge(S["m_qn"], 6)
            hq = Hf1[:, :, :].rearrange("p a (b t) -> p (a b) t", t=T)
            nc.scalar.activation(hq[:, 0:8, :], mq[:, 0:8, :], ACT.Square).then_inc(S["m_qsq"], 1)
            nc.scalar.activation(hq[:, 8:12, :], mq[:, 8:12, :], ACT.Square).then_inc(S["m_qsq"], 1)
            act.wait_ge(S["m_qrv"], 1)
            nc.scalar.activation(mrq[:, :, :], mrq[:, :, :], ACT.Sqrt).then_inc(S["m_qrstd"], 1)
            act.wait_ge(S["m_kn"], 2)
            nc.scalar.activation(Hf1[:, :, :], kn[:, :, :], ACT.Square).then_inc(S["m_ksq"], 1)
            act.wait_ge(S["m_krv"], 1)
            nc.scalar.activation(Hf1[:, :, :], Hf1[:, :, :], ACT.Sqrt).then_inc(S["m_krstd"], 1)

            def exps(h):
                for qt in range(2):
                    act.wait_ge(S["a_max"], 2 * h + qt + 1)
                    if h >= 2:
                        act.wait_ge(S["a_t"], 2 * h - 2)
                    nc.scalar.activation(Pm[:, h % 2, qt, :], ps[:, 2 * (h % 2) + qt, :], ACT.Exp, bias=amx[:, h % 2, qt:qt + 1],
                                         accum_out=asum[:, h % 2, qt:qt + 1]).then_inc(S["a_exp"], 1)
            act.wait_ge(S["m_kn2"], 1)
            act.wait_ge(S["m_rot"], 2)
            exps(0)
            for h in range(MH):
                if h + 1 < MH:
                    exps(h + 1)
                for qt in range(2):
                    act.wait_ge(S["a_t"], 2 * h + qt + 1)
                    if h >= 1:
                        act.wait_ge(S["a_o"], h)
                    nc.scalar.activation(PTm[:, :, qt * P:(qt + 1) * P], ps[:, 4 + qt, :].rearrange("p (k q) -> p k q", q=P),
                                         ACT.Copy).then_inc(S["a_pt"], 1)
            out_act(act, "mo")

        def mla_dve(dve):
            for j, (bank, n, ntok) in enumerate(((4, 256, TT), (5, 64, TT), (6, 384, T))):
                dve.wait_ge(S["m_css"], j + 1)
                dlink(nc.vector.tensor_scalar(mrst[:, j, 0:ntok], ps[:, bank, 0:ntok], 1.0 / n, EPS, ALU.mult, ALU.add))
                nc.vector.reciprocal(mrst[:, j, 0:ntok], mrst[:, j, 0:ntok]).then_inc(S["m_crv"], 1)
            for m, (name, j, ntok) in enumerate(MLA_SRC):
                r = {"ckv": 0, "kpe": 1, "cq": 2}[name]
                g = {"ckv": pc("g_kvl", j), "kpe": pc("g_kr"), "cq": pc("g_ql", j)}[name]
                dve.wait_ge(S["m_crstd"], r + 1)
                dve.wait_ge(S["m_dn"], m + 1)
                nc.vector.scalar_tensor_tensor(mla_dst(m), mla_dst(m), g, mrst[:, r, 0:ntok], ALU.mult, ALU.mult).then_inc(S["m_cn"], 1)
                dve.wait_ge(S["m_cn"], m + 1)
                if name == "kpe":
                    continue
                hi, lo = (ckvhi, ckvlo) if name == "ckv" else (cqhi, cqlo)
                dlink(nc.vector.tensor_copy(hi[:, j, :], mla_dst(m)))
                nc.vector.tensor_tensor(lo[:, j, :], mla_dst(m), hi[:, j, :].bitcast(F32), ALU.subtract).then_inc(S["m_clo"], 1)
            for j in range(2):
                dve.wait_ge(S["slot_used"], START["uv"] + j + 1)
                b = 4 if j == 0 else 0
                nc.vector.tensor_copy(mv[:, :, j * 512:(j + 1) * 512], ps[:, b:b + 4, :]).then_inc(S["m_v"], 1)
            dlink(nc.vector.tensor_scalar(gsc[:, :], par[:, PCOL["g_qn"]:PCOL["g_qn"] + 2], 192.0 ** -0.5, None, ALU.mult))
            dve.wait_ge(S["m_qss"], 6)
            nc_ = nc.vector.tensor_scalar(mrq[:, 0:4, :], ps[:, 0:4, :], 1.0 / 128, EPS, ALU.mult, ALU.add)
            dlink(nc_)
            dlink(nc.vector.tensor_scalar(mrq[:, 4:6, :], ps[:, 4:6, :], 1.0 / 64, EPS, ALU.mult, ALU.add))
            nc.vector.reciprocal(mrq[:, :, :], mrq[:, :, :]).then_inc(S["m_qrv"], 1)
            dve.wait_ge(S["m_qrstd"], 1)
            rq = mrq[:, :, :].rearrange("p a (b t) -> p (a b) t", t=T)
            dlink(nc.vector.scalar_tensor_tensor(mq[:, 0:8, :], mq[:, 0:8, :], gsc[:, 0:1], rq[:, 0:8, :], ALU.mult, ALU.mult))
            dlink(nc.vector.scalar_tensor_tensor(mq[:, 8:12, :], mq[:, 8:12, :], gsc[:, 1:2], rq[:, 8:12, :], ALU.mult, ALU.mult))
            dve.wait_ge(S["m_kss"], 8)
            dlink(nc.vector.tensor_scalar(Hf1[:, :, :], ps[:, :, :], 1.0 / 128, EPS, ALU.mult, ALU.add))
            nc.vector.reciprocal(Hf1[:, :, :], Hf1[:, :, :]).then_inc(S["m_krv"], 1)
            dve.wait_ge(S["m_krstd"], 1)
            nc.vector.scalar_tensor_tensor(kn[:, :, :], kn[:, :, :], pc("g_kn"), Hf1[:, :, :], ALU.mult, ALU.mult).then_inc(S["m_kn2"], 1)
            dve.wait_ge(S["m_sw"], 3)
            dve.wait_ge(S["mlac"], 16)
            cos, sin = mlac[:, P:P + T], mlac[:, P + T:P + 2 * T]
            x, y, tmp = mq[:, 8:12, :], ps[:, 5:7, :].rearrange("p a (b t) -> p (a b) t", t=T), mrq[:, 0:2, :].rearrange("p a (b t) -> p (a b) t", t=T)
            dlink(nc.vector.tensor_tensor(tmp, y, sin.rearrange("p (a t) -> p a t", a=1).to_broadcast([P, 4, T]), ALU.mult))
            dlink(nc.vector.tensor_tensor(x, x, cos.rearrange("p (a t) -> p a t", a=1).to_broadcast([P, 4, T]), ALU.mult))
            nc.vector.tensor_tensor(x, x, tmp, ALU.add).then_inc(S["m_rot"], 1)
            dlink(nc.vector.tensor_tensor(mrst[:, 0, 0:T], ps[:, 7, 0:T], sin, ALU.mult))
            dlink(nc.vector.tensor_tensor(kpe[:, T:TT], kpe[:, T:TT], cos, ALU.mult))
            nc.vector.tensor_tensor(kpe[:, T:TT], kpe[:, T:TT], mrst[:, 0, 0:T], ALU.add).then_inc(S["m_rot"], 1)

            def maxes(h):
                for qt in range(2):
                    dve.wait_ge(S["a_s"], 2 * h + qt + 1)
                    nc.vector.tensor_reduce(amx[:, h % 2, qt:qt + 1], ps[:, 2 * (h % 2) + qt, :], AX_X, ALU.max, negate=True).then_inc(S["a_max"], 1)

            def split_out(h):
                dve.wait_ge(S["a_o"], h + 1)
                nc.vector.tensor_copy(Hhi[:, h, 0:T], ps[:, 6 + h % 2, 0:T]).then_inc(S["a_oh"], 1)
                dve.wait_ge(S["a_oh"], 2 * h + 1)
                nc.vector.tensor_tensor(Hlo[:, h, 0:T], ps[:, 6 + h % 2, 0:T], Hhi[:, h, 0:T].bitcast(F32), ALU.subtract).then_inc(S["a_oh"], 1)
            maxes(0)
            for h in range(MH):
                if h + 1 < MH:
                    maxes(h + 1)
                dve.wait_ge(S["a_exp"], 2 * h + 2)
                dlink(nc.vector.reciprocal(arec[:, h % 2, :], asum[:, h % 2, :]))
                for qt in range(2):
                    x = Pm[:, h % 2, qt, :]
                    nc.vector.tensor_scalar(x, x, arec[:, h % 2, qt:qt + 1], None, ALU.mult).then_inc(S["a_pn"], 1)
                if h >= 1:
                    split_out(h - 1)
            split_out(MH - 1)
            out_dve(dve, "mo", T, (1, 2), S["mo_x"])

        SEC_SRC = [("sqk", j) for j in range(8)] + [("sglu", j) for j in range(4)] + [("sqm", j) for j in range(2)] + [("mk", j) for j in range(2)]
        NB = AH + MEMH

        def sec_pe(pe):
            xhi, xlo = H(T, T)
            pe.wait_ge(*normed("smix"))

            def tiles(a0, a1, hi, lo):
                for a in range(a0, a1):
                    if a >= 4:
                        pe.wait_ge(S["s_ev"], a - 3)
                    name, j = SEC_SRC[a]
                    column_tile(pe, START[name] + j, a % 4, hi, lo, T)
            tiles(0, 8, xhi, xlo)
            for kp in range(4):
                his, los = [], []
                for k2 in range(2):
                    k = 2 * kp + k2
                    for tt in range(2):
                        o = ps[:, 4 + tt, :]
                        a, b = (x[:, k, T + tt * P:T + (tt + 1) * P] for x in (Hhi, Hlo))
                        his.append((o, k2 * 512, 512, False, a, k == 0, False))
                        his.append((o, k2 * 512, 512, False, b, False, False))
                        los.append((o, k2 * 512, 512, False, a, False, k == KD - 1))
                slot_products(pe, START["sv"] + kp, 0, his, los)
            tiles(8, 14, xhi, xlo)
            pe.wait_ge(*normed("smem"))
            tiles(14, 16, lambda k: memhi[:, k, :], lambda k: memlo[:, k, :])
            for kq in range(2):
                his, los = [], []
                for k4 in range(4):
                    k = 4 * kq + k4
                    for tt in range(2):
                        o = ps[:, 6 + tt, 0:T]
                        a, b = (x[:, k, tt * P:(tt + 1) * P] for x in (memhi, memlo))
                        his.append((o, k4 * T, T, False, a, k == 0, False))
                        his.append((o, k4 * T, T, False, b, False, False))
                        los.append((o, k4 * T, T, False, a, False, k == KD - 1))
                slot_products(pe, START["mv"] + kq, 0, his, los)
            pe.wait_ge(S["s_qsq"], 1)
            pe.wait_ge(S["s_ev"], 16)
            pe.wait_ge(S["s_vc"], 1)
            q2 = sqs[:, :, :].rearrange("p (a b) t -> p a (b t)", b=2)
            for j in range(6):
                mm = nc.tensor.matmul(ps[:, j, :], blk64, q2[:, j, :], start=True, stop=True)
            mm.then_inc(S["s_qss"], 1)
            pe.wait_ge(S["s_qn"], 4)
            pe.wait_ge(S["secc"], 16)
            x2 = sq_[:, :, :].rearrange("p (a b) t -> p a (b t)", b=2)
            for j in range(4):
                mm = nc.tensor.matmul(ps[:, j, :], secc[:, 0:P], x2[:, j, :], start=True, stop=True)
            mm.then_inc(S["s_sw"], 1)
            pe.wait_ge(S["s_glu"], 62)
            pe.wait_ge(S["s_vc"], 2)
            for j in range(2):
                mm = nc.tensor.matmul(ps[:, 6, 0:T], ones, cacc[:, j, :], start=j == 0, stop=j == 1)
            mm.then_inc(S["s_mu"], 1)
            pe.wait_ge(S["s_csq"], 2)
            for j in range(2):
                mm = nc.tensor.matmul(ps[:, 7, 0:T], ones, csq[:, j, :], start=j == 0, stop=j == 1)
            mm.then_inc(S["s_cvs"], 1)
            pe.wait_ge(S["s_rot"], 1)
            pe.wait_ge(S["s_cn"], 2)

            def scores(a):
                r = slice(64 * (a % 2), 64 * (a % 2) + 64)
                tq, tk = (a // 2, 4 + a // 2) if a < AH else (8 + (a - AH) // 2, 10 + (a - AH) // 2)
                if a >= 2:
                    pe.wait_ge(S["b_exp"], 2 * (a - 1))
                for qt in range(2):
                    mm = nc.tensor.matmul(ps[:, a % 2, qt * T:(qt + 1) * T], sq_[r, tq, qt * P:(qt + 1) * P], sq_[r, tk, :], start=True, stop=True)
                mm.then_inc(S["b_s"], 1)
            scores(0)
            for a in range(NB):
                if a + 1 < NB:
                    scores(a + 1)
                pe.wait_ge(S["b_pn"], a + 1)
                if a >= 2:
                    pe.wait_ge(S["b_pt"], a - 1)
                for qt in range(2):
                    for kt in range(2):
                        c = (2 * qt + kt) * P
                        mm = nc.tensor.transpose(ps[:, 2 + a % 2, c:c + P], Pb[:, a % 2, qt, kt * P:(kt + 1) * P], ident)
                mm.then_inc(S["b_t"], 1)
                pe.wait_ge(S["b_pt"], a + 1)
                j = a // 2
                if j >= 2 and a % 2 == 0:
                    pe.wait_ge(S["b_oh"], 2 * (j - 1))
                r0 = 64 * (a % 2)
                for kt in range(2):
                    v = svt[:, kt, a * 64:(a + 1) * 64] if a < AH else svm[:, kt, (a - AH) * 64:(a - AH + 1) * 64]
                    mm = nc.tensor.matmul(ps[r0:r0 + 64, 4 + j % 2, 0:T], v, PTb[:, a % 2, kt, :], start=kt == 0, stop=kt == 1)
                mm.then_inc(S["b_o"], 1)
            out_pe(pe, "so", lambda k: Hhi[:, k, 0:T], lambda k: Hlo[:, k, 0:T], T, S["so_x"], [(S["b_oh"], 12), (S["s_ch"], 4)])

        def sec_act(act):
            def evac(a):
                name, j = SEC_SRC[a]
                n = START[name] + j
                act.wait_ge(S["slot_used"], n + 1)
                src = ps[:, a % 4, 0:T]
                if name == "sglu":
                    dst, f = (sga[:, j, :], ACT.Copy) if j < 2 else (sgg[:, j - 2, :], ACT.Sigmoid)
                else:
                    dst, f = sq_[:, {"sqk": 0, "sqm": 8, "mk": 10}[name] + j, :], ACT.Copy
                nc.scalar.activation(dst, src, f).then_inc(S["s_ev"], 1)
                hi_slot(act, n + RING)
            for a in range(8):
                evac(a)
            for j in range(4):
                hi_slot(act, START["sv"] + j + RING)
            for a in range(8, 16):
                evac(a)
            for j in range(2):
                hi_slot(act, START["mv"] + j + RING)
            act.wait_ge(S["s_ev"], 16)
            nc.scalar.activation(sqs[:, :, :], sq_[:, :, :], ACT.Square).then_inc(S["s_qsq"], 1)
            act.wait_ge(S["s_qrv"], 1)
            nc.scalar.activation(sqs[:, :, :], sqs[:, :, :], ACT.Sqrt).then_inc(S["s_qrstd"], 1)
            act.wait_ge(S["t_tab"], 1)
            nc.scalar.activation(tab[:, 0:2, :], tab[:, 0:2, :], ACT.Sin).then_inc(S["t_sin"], 1)
            act.wait_ge(S["s_xc"], 2)
            for j in range(2):
                nc.scalar.activation(csq[:, j, :], cacc[:, j, :], ACT.Square).then_inc(S["s_csq"], 1)
            act.wait_ge(S["s_crv"], 1)
            nc.scalar.activation(crst[:, 0, :], crst[:, 0, :], ACT.Sqrt).then_inc(S["s_crstd"], 1)
            act.wait_ge(S["s_cn"], 2)
            for j in range(2):
                nc.scalar.activation(csq[:, j, :], cacc[:, j, :], ACT.Silu, scale=pc("ln_g", j), bias=pc("ln_b", j)).then_inc(S["s_cs"], 1)

            def exps(a):
                for qt in range(2):
                    act.wait_ge(S["b_max"], a + 1)
                    if a >= 2:
                        act.wait_ge(S["b_t"], a - 1)
                    src = Sb[:, a % 2, qt, :] if a < AH else ps[:, a % 2, qt * T:(qt + 1) * T]
                    nc.scalar.activation(Pb[:, a % 2, qt, :], src, ACT.Exp, bias=bmx[:, a % 2, qt:qt + 1],
                                         accum_out=bsum[:, a % 2, qt:qt + 1]).then_inc(S["b_exp"], 1)
            exps(0)
            for a in range(NB):
                if a + 1 < NB:
                    exps(a + 1)
                act.wait_ge(S["b_t"], a + 1)
                if a >= 2:
                    act.wait_ge(S["b_o"], a - 1)
                nc.scalar.activation(PTb[:, a % 2, :, :].rearrange("p k (q t) -> p q k t", t=P),
                                     ps[:, 2 + a % 2, :].rearrange("p (q k t) -> p q k t", q=2, k=2), ACT.Copy).then_inc(S["b_pt"], 1)
            out_act(act, "so")

        def sec_dve(dve):
            dve.wait_ge(S["posin"], 16)
            ang, turns, t3 = tab[:, 1, :], tab[:, 2, :], tab[:, 3, :]
            dlink(nc.vector.tensor_copy(t3, posi[:, :]))
            dlink(nc.vector.tensor_scalar(ang, t3, con[:, CCOL["invf"]:CCOL["invf"] + 1], None, ALU.mult))
            dlink(nc.vector.tensor_scalar(turns, ang, float(1 / (2 * np.pi)), 12582912.0, ALU.mult, ALU.add))
            dlink(nc.vector.tensor_scalar(turns, turns, -12582912.0, None, ALU.add))
            c1 = 6.28125
            c2 = float(np.float32(np.float64(2 * np.pi) - c1) * 1.0)
            c2 = float(np.frombuffer(np.uint32(np.frombuffer(np.float32(c2).tobytes(), np.uint32)[0] & 0xFFFFF000).tobytes(), np.float32)[0])
            c3 = float(2 * np.pi - c1 - c2)
            for cc in (c1, c2, c3):
                dlink(nc.vector.scalar_tensor_tensor(ang, turns, -cc, ang, ALU.mult, ALU.add))
            PI = 3.1415925
            dlink(nc.vector.tensor_scalar(ang, ang, PI, -PI, ALU.min, ALU.max))
            dlink(nc.vector.scalar_tensor_tensor(t3, ang, -1.0, ang, ALU.mult, ALU.max))
            nc.vector.tensor_scalar(tab[:, 0, :], t3, -1.0, float(np.pi / 2), ALU.mult, ALU.add).then_inc(S["t_tab"], 1)
            dve.wait_ge(S["slot_used"], START["sv"] + 4)
            nc.vector.tensor_copy(svt[:, :, :], ps[:, 4:6, :]).then_inc(S["s_vc"], 1)
            dlink(nc.vector.memset(cpad[:, :, :], 0.0))
            dve.wait_ge(S["s_ev"], 12)
            dlink(nc.vector.tensor_tensor(cpad[:, :, 15:15 + T], sga[:, :, :], sgg[:, :, :], ALU.mult))
            for j in range(2):
                ins = nc.vector.tensor_scalar(cacc[:, j, :], cpad[:, j, 0:T], pc("dw", j), pc("dwb", j), ALU.mult, ALU.add)
                ins.then_inc(S["s_glu"], 1)
            for tap in range(1, 31):
                for j in range(2):
                    dve.wait_ge(S["s_glu"], 2 * (tap - 1) + j + 1)
                    nc.vector.scalar_tensor_tensor(cacc[:, j, :], cpad[:, j, tap:tap + T], pc("dw", 2 * tap + j), cacc[:, j, :],
                                                   ALU.mult, ALU.add).then_inc(S["s_glu"], 1)
            dve.wait_ge(S["s_glu"], 62)
            dve.wait_ge(S["slot_used"], START["mv"] + 2)
            nc.vector.tensor_copy(svm[:, :, :], ps[:, 6:8, 0:T]).then_inc(S["s_vc"], 1)
            dlink(nc.vector.tensor_scalar(gsc2[:, 0:1], pc("g_sq"), 0.125, None, ALU.mult))
            dlink(nc.vector.tensor_scalar(gsc2[:, 1:2], pc("g_smq"), 0.125, None, ALU.mult))
            dve.wait_ge(S["s_qss"], 1)
            q2 = sqs[:, :, :].rearrange("p (a b) t -> p a (b t)", b=2)
            dlink(nc.vector.tensor_scalar(q2, ps[:, 0:6, :], 1.0 / 64, EPS, ALU.mult, ALU.add))
            nc.vector.reciprocal(sqs[:, :, :], sqs[:, :, :]).then_inc(S["s_qrv"], 1)
            dve.wait_ge(S["s_qrstd"], 1)
            for a, b, g in ((0, 4, gsc2[:, 0:1]), (4, 8, pc("g_sk")), (8, 10, gsc2[:, 1:2]), (10, 12, pc("g_smk"))):
                nc.vector.scalar_tensor_tensor(sq_[:, a:b, :], sq_[:, a:b, :], g, sqs[:, a:b, :], ALU.mult, ALU.mult).then_inc(S["s_qn"], 1)
            dve.wait_ge(S["s_qn"], 4)
            dve.wait_ge(S["s_sw"], 1)
            dve.wait_ge(S["t_sin"], 1)
            x, tmp = sq_[:, 0:8, :], sqs[:, 0:8, :]
            dlink(nc.vector.tensor_tensor(tmp, ps[:, 0:4, :].rearrange("p a (b t) -> p (a b) t", t=T), tab[:, 1:2, :].to_broadcast([P, 8, T]), ALU.mult))
            dlink(nc.vector.tensor_tensor(x, x, tab[:, 0:1, :].to_broadcast([P, 8, T]), ALU.mult))
            nc.vector.tensor_tensor(x, x, tmp, ALU.add).then_inc(S["s_rot"], 1)
            dve.wait_ge(S["s_mu"], 1)
            for j in range(2):
                nc.vector.scalar_tensor_tensor(cacc[:, j, :], ps[:, 6, 0:T], -1.0 / 256, cacc[:, j, :], ALU.mult, ALU.add).then_inc(S["s_xc"], 1)
            dve.wait_ge(S["s_xc"], 2)
            dve.wait_ge(S["s_cvs"], 1)
            dlink(nc.vector.tensor_scalar(crst[:, 0, :], ps[:, 7, 0:T], 1.0 / 256, EPS, ALU.mult, ALU.add))
            nc.vector.reciprocal(crst[:, 0, :], crst[:, 0, :]).then_inc(S["s_crv"], 1)
            dve.wait_ge(S["s_crstd"], 1)
            for j in range(2):
                nc.vector.tensor_tensor(cacc[:, j, :], cacc[:, j, :], crst[:, 0, :], ALU.mult).then_inc(S["s_cn"], 1)

            def split(src, k, signal, count):
                nc.vector.tensor_copy(Hhi[:, k, 0:T], src).then_inc(signal, 1)
                dve.wait_ge(signal, count + 1)
                nc.vector.tensor_tensor(Hlo[:, k, 0:T], src, Hhi[:, k, 0:T].bitcast(F32), ALU.subtract).then_inc(signal, 1)
            for j in range(2):
                dve.wait_ge(S["s_cs"], j + 1)
                split(csq[:, j, :], 4 + j, S["s_ch"], 2 * j)

            def maxes(a):
                dve.wait_ge(S["b_s"], a + 1)
                src = ps[:, a % 2, :].rearrange("p (q k) -> p q k", q=2)
                if a < AH:
                    if a >= 2:
                        dve.wait_ge(S["b_exp"], 2 * (a - 1))
                    nc.vector.tensor_tensor(Sb[:, a % 2, :, :], src, secc[:, P:P + 2 * T].rearrange("p (q k) -> p q k", q=2), ALU.add).then_inc(S["b_sb"], 1)
                    dve.wait_ge(S["b_sb"], a + 1)
                    src = Sb[:, a % 2, :, :]
                nc.vector.tensor_reduce(bmx[:, a % 2, :], src, AX_X, ALU.max, negate=True).then_inc(S["b_max"], 1)

            def split_out(j):
                dve.wait_ge(S["b_o"], 2 * j + 2)
                split(ps[:, 4 + j % 2, 0:T], j if j < 4 else 2 + j, S["b_oh"], 2 * j)
            maxes(0)
            for a in range(NB):
                if a + 1 < NB:
                    maxes(a + 1)
                dve.wait_ge(S["b_exp"], 2 * a + 2)
                dlink(nc.vector.reciprocal(brec[:, a % 2, :], bsum[:, a % 2, :]))
                x = Pb[:, a % 2, :, :]
                nc.vector.tensor_tensor(x, x, brec[:, a % 2, :].rearrange("p (q o) -> p q o", o=1).to_broadcast([P, 2, T]), ALU.mult).then_inc(S["b_pn"], 1)
                if a >= 2 and a % 2 == 0:
                    split_out(a // 2 - 1)
            split_out(NB // 2 - 1)
            out_dve(dve, "so", T, None, S["so_x"])

        def ada_col(L, part_):
            return lambda k, h: ada[L][:, 16 * part_ + 2 * k + h:16 * part_ + 2 * k + h + 1]

        def norms(t):
            full = lambda k: XT[:, k, :]
            half = lambda k: XT[:, k, T:TT]
            dsts = {TT: (lambda k: Hhi[:, k, :], lambda k: Hlo[:, k, :]), T: (lambda k: Hhi[:, k, T:TT], lambda k: Hlo[:, k, T:TT])}
            am_ = lambda L, n: (lambda k, h: amod[L][:, 16 * n + 2 * k + h:16 * n + 2 * k + h + 1])
            am1 = lambda L, n: (lambda k, h: amod[L][:, 16 * n + 2 * k + 1:16 * n + 2 * k + 2])
            ad1 = lambda L, n: (lambda k, h: ada[L][:, 16 * n + 2 * k + 1:16 * n + 2 * k + 2])
            g = lambda name: (lambda k, h: pc(name, k))
            return {
                "mix0": (full, lambda k: [(S["xin"], 16), (S["ctxin"], 16), (S["amod0"], 2)], TT, am_(0, 0), ada_col(0, 0), Hf0, *dsts[TT]),
                "ffn0": (full, lambda k: [(S["go_x"], 5 + k)], TT, am_(0, 1), ada_col(0, 3), Hff, *dsts[TT]),
                "mix1": (full, lambda k: [(S["f0_dn"], 12), (S["amod1"], 2)], TT, am_(1, 0), ada_col(1, 0), Hf1, *dsts[TT]),
                "ffn1": (half, lambda k: [(S["mo_x"], 5 + k)], T, am1(1, 1), ad1(1, 3), Hff, *dsts[T]),
                "smix": (half, lambda k: [(S["f1_dn"], 5 + k)], T, g("g_smix"), None, Hf2, *dsts[T]),
                "smem": (lambda k: memx[:, k, :], lambda k: [(S["memin"], 16), normed("smix")], T, g("g_mem"), None, Hf2,
                         lambda k: memhi[:, k, :], lambda k: memlo[:, k, :]),
                "sffn": (half, lambda k: [(S["so_x"], 5 + k)], T, g("g_sffn"), None, Hff, *dsts[T]),
            }

        PROGRAM = ["ada0", "mix0", "gla", "ffn0", "f0", "ada1", "mix1", "mla", "ffn1", "f1", "smix", "smem", "sec", "sffn", "f2"]
        LAST = S["f2_dn"]
        END_SLOT = NSLOTS

        def tensor_program(pe):
            for st in PROGRAM:
                if st in ("ada0", "ada1"):
                    ada_pe(pe, int(st[-1]), row0 if st == "ada0" else adarow1)
                elif st == "gla":
                    gla_pe(pe)
                elif st == "mla":
                    mla_pe(pe)
                elif st == "sec":
                    sec_pe(pe)
                elif st in ("f0", "f1", "f2"):
                    pe.wait_ge(*normed({"f0": "ffn0", "f1": "ffn1", "f2": "sffn"}[st]))
                    ffn_pe(pe, int(st[-1]), TT if st == "f0" else T)
                else:
                    a = norms(st)[st]
                    norm_pe(pe, st, a[2], a[5])

        def scalar_program(act):
            for st in PROGRAM:
                if st in ("ada0", "ada1"):
                    ada_act(act, int(st[-1]))
                elif st == "gla":
                    gla_act(act)
                elif st == "mla":
                    mla_act(act)
                elif st == "sec":
                    sec_act(act)
                elif st in ("f0", "f1", "f2"):
                    ffn_act(act, int(st[-1]), TT if st == "f0" else T)
                else:
                    if st == "mix1":
                        act.wait_ge(S["f0_dn"], 12)
                        act.dma_start(mlac[:, :], mla_c).then_inc(S["mlac"], 16)
                    if st == "smix":
                        act.wait_ge(S["f1_dn"], 12)
                        for dst, src, name in ((memx[:, :, :], mem_in, "memin"), (posi[:, :], pos_in, "posin"), (secc[:, :], sec_c, "secc")):
                            act.dma_start(dst, src).then_inc(S[name], 16)
                    a = norms(st)[st]
                    norm_act(act, st, *a[:6])

        def vector_program(dve):
            for st in PROGRAM:
                if st in ("ada0", "ada1"):
                    ada_dve(dve, int(st[-1]), row0 if st == "ada0" else adarow1)
                elif st == "gla":
                    gla_dve(dve)
                elif st == "mla":
                    mla_dve(dve)
                elif st == "sec":
                    sec_dve(dve)
                elif st in ("f0", "f1", "f2"):
                    ffn_dve(dve, int(st[-1]), TT if st == "f0" else T, {"f0": (0, 5), "f1": (1, 5), "f2": None}[st])
                else:
                    a = norms(st)[st]
                    norm_dve(dve, st, a[0], a[2], a[5], a[6], a[7])

        def sync_tail(sp):
            sp.wait_ge(LAST, 12)
            sp.dma_start(out, XT[:, :, T:TT]).then_inc(S["outd"], 16)
            sp.wait_ge(S["outd"], 16)
            for name in ("parin", "constin", "xin", "ctxin", "glac", "w2in"):
                sp.wait_ge(S[name], 16)

        @block.sync
        def _(sp):
            for dst, src, name in ((par, params, "parin"), (con, consts, "constin")):
                sp.dma_start(dst[:, :], src).then_inc(S[name], 16)
            for n in range(RING):
                load_slot(sp, n)
            sp.dma_start(XT[:, :, T:TT], x_in).then_inc(S["xin"], 16)
            sp.dma_start(XT[:, :, 0:T], ctx_in).then_inc(S["ctxin"], 16)
            sp.dma_start(glac[:, :], gla_c).then_inc(S["glac"], 16)
            sp.dma_start(w2[:, :], w2_in).then_inc(S["w2in"], 16)
            loops = (END_SLOT - RING) // RING
            with sp.Fori(0, loops) as i:
                for j in range(RING):
                    load_slot(sp, RING + j, i * RING)
            for n in range(RING + loops * RING, END_SLOT):
                load_slot(sp, n)
            sync_tail(sp)

        @block.gpsimd
        def _(pool):
            for n in range(RING):
                lo_slot(pool, n)
            loops = (END_SLOT - RING) // RING
            with pool.Fori(0, loops) as i:
                for j in range(RING):
                    lo_slot(pool, RING + j, i * RING)
            for n in range(RING + loops * RING, END_SLOT):
                lo_slot(pool, n)

        @block.tensor
        def _(pe):
            pe.wait_ge(S["constin"], 16)
            tensor_program(pe)

        @block.scalar
        def _(act):
            act.wait_ge(S["parin"], 16)
            nc.scalar.activation(amod[0][:, 0:16], pc("c", 0, 16), ACT.Silu).then_inc(S["csil"], 1)
            for n in range(RING):
                hi_slot(act, n)
            scalar_program(act)

        @block.vector
        def _(dve):
            dlink(nc.vector.memset(c4[:, :, :].bitcast(F32), 0.0))
            dve.wait_ge(S["csil"], 1)
            cs = amod[0][:, 0:16].rearrange("p (k v) -> p k v", v=2)
            nc.vector.tensor_copy(c4[:, :, 0:2], cs).then_inc(S["c4"], 1)
            dve.wait_ge(S["c4"], 1)
            nc.vector.tensor_tensor(c4[:, :, 2:4], cs, c4[:, :, 0:2].bitcast(F32), ALU.subtract).then_inc(S["c4"], 1)
            dve.wait_ge(S["c4"], 2)
            vector_program(dve)

def _columns(a):
    return np.asarray(a).reshape(-1, P).T


def _tile(w):
    return np.asarray(w).reshape(-1, P, w.shape[-1]).transpose(1, 0, 2).reshape(P, -1)


def _pad(a, width=1024):
    return np.concatenate([a, np.zeros((P, width - a.shape[1]), a.dtype)], axis=1) if a.shape[1] < width else a


def _stream(v):
    got = []

    def put(*parts):
        got.append(_pad(np.concatenate(parts, axis=1) if len(parts) > 1 else parts[0]))

    def column_tiles(w, c0, count):
        for j in range(count):
            put(_tile(w[:, c0 + j * P:c0 + (j + 1) * P]))

    def ada_slots(w):
        for q in range(6):
            for k in range(KD):
                put(w[k * P:(k + 1) * P, q * 1024:(q + 1) * 1024])

    def ffn(up, down, a0, g0):
        for i in range(FF_T):
            column_tiles(up, a0 + i * P, 1)
            column_tiles(up, g0 + i * P, 1)
        for m in range(KD):
            for k0, k1 in ((0, 8), (8, 16), (16, 22)):
                put(_tile(down[k0 * P:k1 * P, m * P:(m + 1) * P]))

    half = FF_T * P
    ada_slots(v["w_ada"][0])
    w1 = v["gla_gate_w1"][0]
    gate = np.zeros((D, P), w1.dtype)
    gate[:, 0:16], gate[:, 32:48] = w1[0], w1[1]
    put(_tile(gate))
    w = v["gla_w_in"][0]
    column_tiles(w, 0, 8)
    for c in range(2):
        for k in range(0, KD, 2):
            put(_tile(w[k * P:(k + 2) * P, 1024 + c * 512:1024 + (c + 1) * 512]))
    column_tiles(w, 2048, 8)
    column_tiles(v["gla_w_out"][0], 0, 8)
    ffn(v["ffn_w_up"][0], v["ffn_w_down"][0], 0, half)
    ada_slots(v["w_ada"][1])
    w = v["mla_w_down"][0]
    column_tiles(w, 384, 2)
    put(_tile(np.concatenate([w[:, 640:704], w[:, 640:704]], axis=1)))
    column_tiles(w, 0, 3)
    w = v["mla_w_uq"][0]
    tiles = [w[:, h * 192:h * 192 + P] for h in range(MH)]
    tiles += [np.concatenate([w[:, h * 192 + P:(h + 1) * 192] for h in (j, j + 1)], axis=1) for j in range(0, MH, 2)]
    for j in range(0, 12, 2):
        put(_tile(tiles[j]), _tile(tiles[j + 1]))
    w = v["mla_w_ukv"][0]
    for j in range(0, MH, 4):
        put(*[_tile(w[:, h * 256:h * 256 + P]) for h in range(j, j + 4)])
    for j in range(0, MH, 4):
        put(_tile(np.concatenate([w[:, h * 256 + P:(h + 1) * 256] for h in range(j, j + 4)], axis=1)))
    column_tiles(v["mla_w_out"][0], 0, 8)
    ffn(v["ffn_w_up"][1], v["ffn_w_down"][1], 0, half)
    w = v["w_in_2"][0]
    column_tiles(w, 0, 8)
    for k in range(0, KD, 2):
        put(_tile(w[k * P:(k + 2) * P, 1024:1536]))
    column_tiles(w, 1536, 4)
    column_tiles(w, 2048, 2)
    w = v["w_mem_kv_2"][0]
    column_tiles(w, 0, 2)
    for k in range(0, KD, 4):
        put(_tile(w[k * P:(k + 4) * P, 256:512]))
    column_tiles(v["w_out_2"][0], 0, 8)
    ffn(v["w_up_2"][0], v["w_down_2"][0], half, 0)
    assert len(got) == NSLOTS
    return np.stack(got)


def _params(v):
    twice = lambda a: np.repeat(a, 2, axis=1)
    both = lambda a: np.concatenate([a, a])[:, None]
    p = {"c": np.stack([_columns(v["c_ctx"]), _columns(v["c"][0])], axis=2).reshape(P, 16)}
    for L in (0, 1):
        p[f"b_ada{L}"] = twice(_columns(v["b_ada"][L]))
        p[f"g_mix{L}"] = twice(_columns(v["norm_mix"][L]))
        p[f"g_ffn{L}"] = twice(_columns(v["norm_ffn"][L]))
    p["gate_b"] = np.asarray(v["gla_gate_b"][0]).reshape(2, GH, P).transpose(2, 1, 0).reshape(P, 8)
    p["g_out"], p["g_ql"], p["g_kvl"] = (_columns(v[n][0]) for n in ("gla_out_norm", "mla_q_lora_norm", "mla_kv_lora_norm"))
    for n, src in (("q", "mla_q_norm"), ("k", "mla_k_norm")):
        p[f"g_{n}n"], p[f"g_{n}r"] = v[src][0][:P, None], both(v[src][0][P:])
    half = FF_T * P

    def by_slot(a, swapped):
        x, y = _columns(a[:half]), _columns(a[half:])
        return np.stack([y, x] if swapped else [x, y], axis=2).reshape(P, 2 * FF_T)
    for f, (cw, cb) in enumerate(((v["ffn_conv_w"][0], v["ffn_conv_b"][0]), (v["ffn_conv_w"][1], v["ffn_conv_b"][1]),
                                  (v["ffn_dw_w_2"][0], v["ffn_dw_b_2"][0]))):
        for t in range(3):
            p[f"cw{f}_{t}"] = by_slot(cw[t], f == 2)
        p[f"cb{f}"] = by_slot(cb, f == 2)
    for n, src in (("g_smix", "mix_norm_g_2"), ("g_mem", "mem_norm_g_2"), ("dwb", "conv_dw_b_2"), ("ln_g", "conv_ln_g_2"),
                   ("ln_b", "conv_ln_b_2"), ("g_sffn", "ffn_norm_g_2")):
        p[n] = _columns(v[src][0])
    for n, src in (("g_sq", "q_norm_g_2"), ("g_sk", "k_norm_g_2"), ("g_smq", "mq_norm_g_2"), ("g_smk", "mk_norm_g_2")):
        p[n] = both(v[src][0])
    p["dw"] = np.concatenate([_columns(row) for row in v["conv_dw_w_2"][0]], axis=1)
    return np.concatenate([p[n] for n, _ in PARAMS], axis=1)


def _constants():
    f = np.float32
    i, j = np.arange(P)[:, None], np.arange(P)[None, :]
    sel4 = np.zeros((P, 2), f)
    sel4[[0, 2], 0] = sel4[[1, 3], 1] = 1
    inv = np.zeros((P, 1), f)
    freq = (500000.0 ** (-np.arange(0, 16, 2) / 16)).astype(f)
    swap2 = np.zeros((P, P), f)
    for b in (0, 64):
        inv[b:b + 8, 0], inv[b + 8:b + 16, 0] = -freq, freq
        for n in range(8):
            swap2[b + n, b + 8 + n] = swap2[b + 8 + n, b + n] = 1
    con = np.concatenate([np.eye(P), np.ones((P, P)), i // 64 == j // 64, sel4, inv], axis=1).astype(f)
    same = i // CH == j // CH
    gla = np.concatenate([same & (j >= i), same & (j <= i), np.tile((np.arange(TT) % CH != 0)[None], (P, 1))], axis=1).astype(f)
    t = np.arange(T)
    freq = (10000.0 ** (-np.arange(16) / 16)).astype(f)
    ang = np.stack([(t // 64)[None] * freq[:, None], (t % 64)[None] * freq[:, None]]).astype(f)
    sin, cos = np.sin(ang), np.cos(ang)
    c64 = np.concatenate([cos[0], cos[0], cos[1], cos[1]])
    s64 = np.concatenate([-sin[0], sin[0], -sin[1], sin[1]])
    swap1 = np.zeros((P, P), f)
    for n in range(P):
        swap1[n ^ 16, n] = 1
    mla = np.concatenate([swap1, np.tile(c64, (2, 1)), np.tile(s64, (2, 1))], axis=1).astype(f)
    q, k = t[:, None], t[None, :]
    m = np.zeros((T, T), np.float64)
    for window, dil in ((128, 1), (512, 4), (2048, 16)):
        m += (np.abs(q - k) <= window // 2) & ((q - k) % dil == 0)
    bias = np.where(m > 0, np.log(np.maximum(m, 1)), -1e30).reshape(2, P, T).transpose(1, 0, 2).reshape(P, 2 * T)
    sec = np.concatenate([swap2, bias], axis=1).astype(f)
    return con, gla, mla, sec


def kernel(**inputs):
    import concourse.bacc as bacc
    from concourse.bass_utils import run_bass_kernel_spmd

    v = {n: np.asarray(a) for n, a in inputs.items()}
    con, gla, mla, sec = _constants()
    tokens = lambda a: np.ascontiguousarray(a[0].reshape(T, KD, P).transpose(2, 1, 0))
    w2 = np.zeros((P, TT), v["gla_gate_w2"].dtype)
    w2[0:16], w2[32:48] = v["gla_gate_w2"][0, 0], v["gla_gate_w2"][0, 1]
    arrays = {
        "wstream": _stream(v), "params": np.ascontiguousarray(_params(v)), "consts": con,
        "x_t": tokens(v["x"]), "ctx_t": tokens(v["ctx"]), "mem_t": tokens(v["mem_2"]),
        "positions": np.ascontiguousarray(np.broadcast_to(v["positions_2"], (P, T))),
        "gate_w2": w2, "gla_consts": gla, "mla_consts": mla, "sec_consts": sec,
    }
    nc = bacc.Bacc("TRN2", target_bir_lowering=False, num_devices=1)
    args = [nc.dram_tensor(n, a.shape, mybir.dt.from_np(a.dtype), kind="ExternalInput").ap() for n, a in arrays.items()]
    args.append(nc.dram_tensor("out_t", (P, KD, T), F32, kind="ExternalOutput").ap())
    build(nc, *args)
    r = run_bass_kernel_spmd(nc, [arrays], core_ids=[0])
    return np.ascontiguousarray(r.results[0]["out_t"].transpose(2, 1, 0)).reshape(1, T, D)
```
